# Optimizing a Trainium2 kernel written in Bass

```python
import jax, jax.numpy as jnp
from jax import lax
import numpy as np

D_MODEL = 1024
BATCH = 1
SEQ = 512
DEPTH = 1
DEC_BATCH = 8
DEC_SEQ = 8
PAST_LEN = 4096
PAGE_SIZE = 128

D_MIX = D_MODEL
D_CONV = D_MIX // 2
D_POOL = D_MIX - D_CONV
CONV_HEADS = 8
CONV_WIDTH = 31
POOL_WINDOWS = (2, 4, 8, 16)
POOL_GROUPS = len(POOL_WINDOWS)
POOL_GROUP_DIM = D_POOL // POOL_GROUPS
POOL_MAX = max(POOL_WINDOWS)
D_FF = 2816
N_MOD = 9
HALF = 0.5
EPS = 1e-6

kernel_name = "hybrid_conformer_conv_multiscale_pool_decoder_step"

def _rmsnorm(x, g):
    xf = x.astype(jnp.float32)
    y = xf * lax.rsqrt(jnp.mean(xf * xf, axis=-1, keepdims=True) + EPS)
    return (y * g.astype(jnp.float32)).astype(x.dtype)

def _layernorm(x, g, b):
    xf = x.astype(jnp.float32)
    mu = jnp.mean(xf, axis=-1, keepdims=True)
    var = jnp.mean(jnp.square(xf - mu), axis=-1, keepdims=True)
    y = (xf - mu) * lax.rsqrt(var + EPS)
    return (y * g.astype(jnp.float32) + b.astype(jnp.float32)).astype(x.dtype)

def _swiglu(x, w_up, w_down):
    gu = x @ w_up
    g, u = jnp.split(gu, 2, axis=-1)
    return (jax.nn.silu(g) * u) @ w_down

def _depthwise_causal_conv(u_ext, w_dw, b_dw):
    c = u_ext.shape[-1]
    out = lax.conv_general_dilated(
        u_ext, w_dw[:, None, :], window_strides=(1,), padding='VALID',
        dimension_numbers=('NWC', 'WIO', 'NWC'), feature_group_count=c)
    return out + b_dw

def _pool_mix(u_ext, pos0, w_pool, pool_scale):
    bsz, text, _ = u_ext.shape
    t = text - (POOL_MAX - 1)
    uf = u_ext.astype(jnp.float32)
    s0 = jnp.concatenate([jnp.zeros((bsz, 1, D_POOL), jnp.float32), jnp.cumsum(uf, axis=1)], axis=1)
    pos = pos0 + jnp.arange(t, dtype=jnp.int32)
    u_cur = uf[:, POOL_MAX - 1:]
    outs = []
    for gi, w in enumerate(POOL_WINDOWS):
        sl = slice(gi * POOL_GROUP_DIM, (gi + 1) * POOL_GROUP_DIM)
        win_sum = s0[:, POOL_MAX:POOL_MAX + t, sl] - s0[:, POOL_MAX - w:POOL_MAX - w + t, sl]
        count = jnp.minimum(pos + 1, w).astype(jnp.float32)[None, :, None]
        outs.append(win_sum / count - u_cur[:, :, sl])
    pooled = jnp.stack(outs, axis=2).astype(u_ext.dtype)
    mixed = jnp.einsum('btgc,gcd->btgd', pooled, w_pool)
    return mixed.reshape(bsz, t, D_POOL) * pool_scale

def _layer(x, c, conv_prev, pool_prev, pos0,
           w_ada, b_ada, g_ffn1, w_ffn1_up, w_ffn1_down, g_mix, w_in, w_dw, b_dw,
           ln_g, ln_b, w_pool, pool_scale, w_out, g_ffn2, w_ffn2_up, w_ffn2_down):
    bsz = x.shape[0]
    mod = (jax.nn.silu(c) @ w_ada + b_ada).reshape(bsz, N_MOD, 1, D_MODEL)
    sh1, sc1, gt1 = mod[:, 0], mod[:, 1], mod[:, 2]
    shm, scm, gtm = mod[:, 3], mod[:, 4], mod[:, 5]
    sh2, sc2, gt2 = mod[:, 6], mod[:, 7], mod[:, 8]

    x = x + HALF * gt1 * _swiglu(_rmsnorm(x, g_ffn1) * (1 + sc1) + sh1, w_ffn1_up, w_ffn1_down)

    hm = _rmsnorm(x, g_mix) * (1 + scm) + shm
    proj = hm @ w_in
    a = proj[..., :D_CONV]
    g = proj[..., D_CONV:2 * D_CONV]
    u_pool = proj[..., 2 * D_CONV:]
    u_conv = a * jax.nn.sigmoid(g)
    conv_ext = jnp.concatenate([conv_prev, u_conv], axis=1)
    v = _depthwise_causal_conv(conv_ext, w_dw, b_dw)
    v = jax.nn.silu(_layernorm(v, ln_g, ln_b))
    pool_ext = jnp.concatenate([pool_prev, u_pool], axis=1)
    p = _pool_mix(pool_ext, pos0, w_pool, pool_scale)
    mix = jnp.concatenate([v, p], axis=-1) @ w_out
    x = x + gtm * mix

    x = x + HALF * gt2 * _swiglu(_rmsnorm(x, g_ffn2) * (1 + sc2) + sh2, w_ffn2_up, w_ffn2_down)
    return x, conv_ext[:, -(CONV_WIDTH - 1):], pool_ext[:, -(POOL_MAX - 1):]

def setup_inputs(seed: int = 0) -> dict:
    key = jax.random.key(seed)
    ks = jax.random.split(key, 26)

    def nrm(k, shape, scale=1.0):
        return jax.random.normal(k, shape, jnp.float32) * scale

    def gain(k, shape):
        return 1.0 + nrm(k, shape, 0.05)

    return {
        "x_prompt": nrm(ks[0], (BATCH, SEQ, D_MODEL)),
        "x_sample": nrm(ks[1], (DEC_BATCH, DEC_SEQ, D_MODEL)),
        "state_conv": nrm(ks[2], (DEPTH, DEC_BATCH, CONV_WIDTH - 1, D_CONV), 0.5),
        "state_pool": nrm(ks[3], (DEPTH, DEC_BATCH, POOL_MAX - 1, D_POOL)),
        "c_prompt": nrm(ks[4], (BATCH, D_MODEL)),
        "c_sample": nrm(ks[5], (DEC_BATCH, D_MODEL)),
        "w_ada": nrm(ks[6], (DEPTH, D_MODEL, N_MOD * D_MODEL), 0.02),
        "b_ada": nrm(ks[7], (DEPTH, N_MOD * D_MODEL), 0.01),
        "g_ffn1": gain(ks[8], (DEPTH, D_MODEL)),
        "w_ffn1_up": nrm(ks[9], (DEPTH, D_MODEL, 2 * D_FF), D_MODEL ** -0.5),
        "w_ffn1_down": nrm(ks[10], (DEPTH, D_FF, D_MODEL), D_FF ** -0.5),
        "g_mix": gain(ks[11], (DEPTH, D_MODEL)),
        "w_in": nrm(ks[12], (DEPTH, D_MODEL, 2 * D_CONV + D_POOL), D_MODEL ** -0.5),
        "w_dw": nrm(ks[13], (DEPTH, CONV_WIDTH, D_CONV), CONV_WIDTH ** -0.5),
        "b_dw": nrm(ks[14], (DEPTH, D_CONV), 0.01),
        "ln_g": gain(ks[15], (DEPTH, D_CONV)),
        "ln_b": nrm(ks[16], (DEPTH, D_CONV), 0.01),
        "w_pool": nrm(ks[17], (DEPTH, POOL_GROUPS, POOL_GROUP_DIM, POOL_GROUP_DIM), POOL_GROUP_DIM ** -0.5),
        "pool_scale": gain(ks[18], (DEPTH, D_POOL)),
        "w_out": nrm(ks[19], (DEPTH, D_MIX, D_MODEL), D_MIX ** -0.5),
        "g_ffn2": gain(ks[20], (DEPTH, D_MODEL)),
        "w_ffn2_up": nrm(ks[21], (DEPTH, D_MODEL, 2 * D_FF), D_MODEL ** -0.5),
        "w_ffn2_down": nrm(ks[22], (DEPTH, D_FF, D_MODEL), D_FF ** -0.5),
        "g_final": gain(ks[23], (D_MODEL,)),
    }

def reference(x_prompt, x_sample, state_conv, state_pool, c_prompt, c_sample,
              w_ada, b_ada, g_ffn1, w_ffn1_up, w_ffn1_down, g_mix, w_in, w_dw, b_dw,
              ln_g, ln_b, w_pool, pool_scale, w_out, g_ffn2, w_ffn2_up, w_ffn2_down, g_final):
    h_p, h_s = x_prompt, x_sample
    conv_p, pool_p, conv_s, pool_s = [], [], [], []
    for l in range(DEPTH):
        params = (w_ada[l], b_ada[l], g_ffn1[l], w_ffn1_up[l], w_ffn1_down[l], g_mix[l], w_in[l],
                  w_dw[l], b_dw[l], ln_g[l], ln_b[l], w_pool[l], pool_scale[l], w_out[l],
                  g_ffn2[l], w_ffn2_up[l], w_ffn2_down[l])
        bp = h_p.shape[0]
        zero_conv = jnp.zeros((bp, CONV_WIDTH - 1, D_CONV), h_p.dtype)
        zero_pool = jnp.zeros((bp, POOL_MAX - 1, D_POOL), h_p.dtype)
        h_p, cp, pp = _layer(h_p, c_prompt, zero_conv, zero_pool, 0, *params)
        h_s, cs, ps = _layer(h_s, c_sample, state_conv[l], state_pool[l], PAST_LEN, *params)
        conv_p.append(cp)
        pool_p.append(pp)
        conv_s.append(cs)
        pool_s.append(ps)
    y_prompt = _rmsnorm(h_p, g_final)
    y_sample = _rmsnorm(h_s, g_final)
    return (y_prompt, y_sample, jnp.stack(conv_p), jnp.stack(pool_p), jnp.stack(conv_s), jnp.stack(pool_s))


_drawn_inputs = setup_inputs


def setup_inputs(seed=0):
    import zlib

    import numpy as np

    out = dict(_drawn_inputs(seed))
    spreads = {}
    factors = {'b_ada': 3.86,
     'g_ffn1': 5.841,
     'b_dw': 8.0,
     'ln_g': 27.686,
     'ln_b': 200.0,
     'pool_scale': 21.685,
     'g_ffn2': 6.014}
    for name, (base, spread) in spreads.items():
        noise = np.random.default_rng([zlib.crc32(name.encode()), seed]).standard_normal(out[name].shape)
        drawn = base * np.exp(spread * noise) if base else spread * noise
        out[name] = __import__('jax').numpy.asarray(drawn.astype(out[name].dtype))
    for name, factor in factors.items():
        out[name] = (out[name] * factor).astype(out[name].dtype)
    return out
```

```python
from contextlib import ExitStack

import concourse.bass as bass
from concourse import mybir

F32 = mybir.dt.float32
F32R = mybir.dt.float32r
ALU = mybir.AluOpType
ACT = mybir.ActivationFunctionType

P = 128
D_MODEL = 1024
SEQ = 512
DEC_BATCH = 8
DEC_SEQ = 8
D_CONV = 512
D_POOL = 512
WIDTH = 31
WINDOWS = (2, 4, 8, 16)
POOL_MAX = max(WINDOWS)
D_FF = 2816
N_MOD = 9
EPS = 1e-6

KD = D_MODEL // P
CONV_CHUNKS = D_CONV // P
GROUPS = len(WINDOWS)
ROWS = 1 + DEC_BATCH
TOKENS = SEQ + DEC_SEQ * DEC_BATCH
HALF = TOKENS // 2
HALF_PROMPT = SEQ // 2
HALF_STEPS = DEC_SEQ // 2

UNIT = 16 * P
FF_PARTS = (8, 8, 6)
FFN_UNITS = sum(FF_PARTS) + len(FF_PARTS) * KD // 2
FFN1 = 0
GLU = FFN1 + FFN_UNITS
POOL_IN = GLU + CONV_CHUNKS
OUT = POOL_IN + GROUPS // 2
FFN2 = OUT + KD // 2
UNITS = FFN2 + FFN_UNITS

CONV_PAD = WIDTH - 1
POOL_PAD = POOL_MAX - 1
CONV_P = CONV_PAD + SEQ
CONV_S = (CONV_PAD + DEC_SEQ) * DEC_BATCH
POOL_P = POOL_PAD + SEQ
POOL_S = (POOL_PAD + DEC_SEQ) * DEC_BATCH
TAPS_PER_LOOP = 5
TAP_GROUPS = (WIDTH - 1) // TAPS_PER_LOOP

ADA_SLOTS = 3
ADA_QUARTERS = 4
ADA_N = D_MODEL // 4
SHIFT = (0, 3, 6)
SCALE = (1, 4, 7)
GATE = (2, 5, 8)

V_ADA, V_G, V_GF = 0, 72, 96
V_LNG, V_LNB, V_BDW, V_PSC = 104, 108, 112, 116
V_WDW = 120
V_COND = V_WDW + CONV_CHUNKS * WIDTH
V_ALL = V_COND + KD * ROWS


def trunk(nc, x_in, w_units, w_ada, w_pool, vectors, conv_state, pool_state,
          y_out, conv_p_out, pool_p_out, conv_s_out, pool_s_out):
    ctx = ExitStack()
    with ctx:
        def sb(name, shape, dt=F32):
            return ctx.enter_context(nc.sbuf_tensor(name, shape, dt))

        def sem(name):
            return ctx.enter_context(nc.semaphore(name))

        with nc.sbuf_tensor("h_hi", [P, 8, TOKENS], F32R) as h_hi, \
                nc.sbuf_tensor("h_lo", [P, 8, TOKENS], F32R) as h_lo:
            pass
        with ExitStack() as under:
            def alias(name, shape, dt=F32):
                return under.enter_context(nc.sbuf_tensor(name, shape, dt))
            conv_p = alias("conv_p", [P, CONV_CHUNKS, CONV_P])
            v = alias("v", [P, CONV_CHUNKS, TOKENS])
            pool_p = alias("pool_p", [P, GROUPS, POOL_P])
            sums = alias("sums", [P, 2, POOL_P + POOL_S])
            wp_hi = alias("wp_hi", [P, GROUPS * P], F32R)
            wp_lo = alias("wp_lo", [P, GROUPS * P], F32R)
        ctx.enter_context(nc.sbuf_tensor("h_room", [P, 2 * 8 * TOKENS], F32))

        x = sb("x", [P, KD, TOKENS])
        hm_hi = sb("hm_hi", [P, KD, TOKENS], F32R)
        hm_lo = sb("hm_lo", [P, KD, TOKENS], F32R)
        w_raw = sb("w_raw", [P, 2, UNIT])
        w_hi = sb("w_hi", [P, 2, UNIT], F32R)
        w_lo = sb("w_lo", [P, 2, UNIT], F32R)
        ada_raw = sb("ada_raw", [P, ADA_SLOTS, 2, D_MODEL])
        vec = sb("vec", [P, V_ALL])
        cond = sb("cond", [P, KD, 32])
        ident = sb("ident", [P, P])
        ones = sb("ones", [P, P])
        small = sb("small", [P, 16])
        ada_rows = sb("ada_rows", [P, ADA_N])
        mod = sb("mod", [P, N_MOD, KD, ROWS])
        gain = sb("gain", [P, 3, KD, ROWS])
        sil = sb("sil", [P, TOKENS])
        full = sb("full", [P, 2, TOKENS])
        sq = sb("sq", [P, 2, TOKENS])
        acc = sb("acc", [P, TOKENS])
        rstd = sb("rstd", [P, TOKENS])
        gated = sb("gated", [P, 2, HALF_STEPS * DEC_BATCH * 2])
        conv_s = sb("conv_s", [P, CONV_CHUNKS, CONV_S])
        pool_s = sb("pool_s", [P, GROUPS, POOL_S])
        wp_raw = sb("wp_raw", [P, GROUPS * P])
        pooled_hi = sb("pooled_hi", [P, 2, TOKENS], F32R)
        pooled_lo = sb("pooled_lo", [P, 2, TOKENS], F32R)
        mean_in = [acc, rstd]
        eps = small[:, 15:16]

        def bank2(name):
            return ctx.enter_context(nc.psum_tensor(name, [P, 2, 512], F32))
        tile_a, tile_b, stat_ps, ada_ps = (bank2(n) for n in ("tile_a", "tile_b", "stat_ps", "ada_ps"))
        tiles = (tile_a, tile_b)

        vec_in, x_in_sem, state_in, wp_in = sem("vec_in"), sem("x_in_sem"), sem("state_in"), sem("wp_in")
        w_raw_ready = [sem("w_raw_ready0"), sem("w_raw_ready1")]
        ada_raw_ready = [sem(f"ada_raw_ready{n}") for n in range(ADA_SLOTS)]
        state_out, y_sent = sem("state_out"), sem("y_sent")
        zeroed, ident_zero, ident_ready, consts_ready, cond_ready = (
            sem("zeroed"), sem("ident_zero"), sem("ident_ready"), sem("consts_ready"), sem("cond_ready"))
        ada_used, ada_copied, ada_turned = sem("ada_used"), sem("ada_copied"), sem("ada_turned")
        mod_step, mod_ready = sem("mod_step"), sem("mod_ready")
        w_hi_ready, w_lo_ready = sem("w_hi_ready"), sem("w_lo_ready")
        tile_done = (sem("tile_a_done"), sem("tile_b_done"))
        tile_read = (sem("tile_a_read"), sem("tile_b_read"))
        h_hi_ready, h_lo_ready = sem("h_hi_ready"), sem("h_lo_ready")
        gate_tmp, x_ready = sem("gate_tmp"), sem("x_ready")
        sq_ready, sq_used, stat_done, std_ready, rstd_ready = (
            sem("sq_ready"), sem("sq_used"), sem("stat_done"), sem("std_ready"), sem("rstd_ready"))
        norm_t, norm_fs, norm_f = sem("norm_t"), sem("norm_fs"), sem("norm_f")
        hm_hi_ready, hm_lo_ready, y_ready = sem("hm_hi_ready"), sem("hm_lo_ready"), sem("y_ready")
        pads_ready, conv_tap = sem("pads_ready"), sem("conv_tap")
        pool_in_ready, pool_step, window_ready, scaled_ready, pooled_ready = (
            sem("pool_in_ready"), sem("pool_step"), sem("window_ready"), sem("scaled_ready"), sem("pooled_ready"))
        wp_hi_ready, wp_lo_ready = sem("wp_hi_ready"), sem("wp_lo_ready")
        pooled_hi_ready, pooled_lo_ready = sem("pooled_hi_ready"), sem("pooled_lo_ready")
        pmix_done, pmix_hi_ready, pmix_lo_ready = sem("pmix_done"), sem("pmix_hi_ready"), sem("pmix_lo_ready")
        ln_sum_done, ln_centred, ln_sq_ready, ln_var_mm = (
            sem("ln_sum_done"), sem("ln_centred"), sem("ln_sq_ready"), sem("ln_var_mm"))
        ln_std_ready, ln_rstd_ready, ln_scaled = sem("ln_std_ready"), sem("ln_rstd_ready"), sem("ln_scaled")
        vmix_full, vmix_hi_ready, vmix_lo_ready = sem("vmix_full"), sem("vmix_hi_ready"), sem("vmix_lo_ready")

        def halves(ps):
            return ps[:, :, 0:HALF]

        def by_half(t):
            return t.rearrange("p (h n) -> p h n", h=2)

        def prompt(t):
            return t[:, :, 0:HALF_PROMPT]

        def sample(t):
            return t[:, :, HALF_PROMPT:HALF]

        def steps(t):
            return t.rearrange("p h (t b) -> p h t b", b=DEC_BATCH)

        def over_steps(rows):
            return rows.unsqueeze(1).unsqueeze(1).broadcast_to([P, 2, HALF_STEPS, DEC_BATCH])

        def split2(t):
            return t.rearrange("p (h n) -> p h n", h=2)

        def col(a, n=1):
            return vec[:, a:a + n]

        def ffn_parts(first_unit, ffn):
            u, out = first_unit, []
            for part, n in enumerate(FF_PARTS):
                before = ffn * sum(FF_PARTS) + sum(FF_PARTS[:part])
                tiles_before = ffn * (len(FF_PARTS) + 1) * KD + part * KD
                out.append((part, n, u, u + n, before, tiles_before))
                u += n + KD // 2
            return out

        FFNS = (ffn_parts(FFN1, 0), ffn_parts(FFN2, 1))
        OUT_TILES = len(FF_PARTS) * KD
        NORM_TILES = (0, OUT_TILES, OUT_TILES + KD, 2 * OUT_TILES + KD)

        def pairs(eng, count, body, first=0):
            if count // 2 - first <= 0:
                return
            with eng.Fori(first, count // 2) as i:
                for side in range(2):
                    body(i * 2 + side, side)

        def first_pair(body):
            for side in range(2):
                body(side, side)

        block = ctx.enter_context(nc.Block())

        @block.sync
        def _(sp):
            sp.dma_start(vec[:], vectors).then_inc(vec_in, 16)
            for c in range(0, KD, 2):
                sp.dma_start(x[:, c:c + 2, :], x_in[:, c:c + 2, :]).then_inc(x_in_sem, 16)
            for a in range(2 * ADA_QUARTERS):
                if a >= ADA_SLOTS:
                    sp.wait_ge(ada_used, a - ADA_SLOTS + 1)
                sp.dma_start(ada_raw[:, a % ADA_SLOTS], w_ada[a]).then_inc(ada_raw_ready[a % ADA_SLOTS], 16)
            for u in range(2):
                sp.dma_start(w_raw[:, u, :], w_units[u]).then_inc(w_raw_ready[u], 16)
            sp.dma_start(conv_s[:, :, 0:CONV_PAD * DEC_BATCH], conv_state).then_inc(state_in, 16)
            sp.dma_start(pool_s[:, :, 0:POOL_PAD * DEC_BATCH], pool_state).then_inc(state_in, 16)
            sp.dma_start(wp_raw[:], w_pool).then_inc(wp_in, 16)
            with sp.Fori(1, UNITS // 2) as i:
                for side in range(2):
                    sp.wait_ge(w_lo_ready, i * 2 + (side - 1))
                    sp.dma_start(w_raw[:, side, :], w_units[i * 2 + side]).then_inc(w_raw_ready[side], 16)
            for c in range(KD):
                sp.wait_ge(y_ready, c + 1)
                sp.dma_start(y_out[:, c, :], x[:, c, :]).then_inc(y_sent, 16)
            sp.wait_ge(y_sent, 16 * KD)
            sp.wait_ge(state_out, 16 * 4)

        @block.tensor
        def _(pe):
            def ada_products(s):
                pe.wait_ge(cond_ready, 1)
                if s >= 2:
                    pe.wait_ge(ada_copied, s - 1)
                for q in range(ADA_QUARTERS):
                    a = ADA_QUARTERS * s + q
                    pe.wait_ge(ada_raw_ready[a % ADA_SLOTS], 16 * (a // ADA_SLOTS + 1))
                    for kk in range(2):
                        k = 2 * q + kk
                        for g in range(4):
                            mm = pe.matmul(ada_ps[32 * g:32 * g + 32, s % 2, 0:ADA_N], cond[:, k, :],
                                           ada_raw[:, a % ADA_SLOTS, kk, ADA_N * g:ADA_N * (g + 1)],
                                           start=(k == 0), stop=(k == KD - 1))
                    mm.then_inc(ada_used, 1)

            def ada_turn(s):
                pe.wait_ge(ada_copied, s + 1)
                pe.wait_ge(ident_ready, 1)
                if s >= 2:
                    pe.wait_ge(mod_ready, s - 1)
                for j in range(2):
                    mm = pe.transpose(ada_ps[:, s % 2, ADA_N + P * j:ADA_N + P * (j + 1)],
                                      ada_rows[:, P * j:P * (j + 1)], ident[:])
                mm.then_inc(ada_turned, 1)

            def passes(ps, w_slot, block_col, hi, lo, k, first, last):
                cols = slice(block_col * P, (block_col + 1) * P)
                for n, (w, r) in enumerate(((w_hi, hi), (w_hi, lo), (w_lo, hi))):
                    for h in range(2):
                        mm = pe.matmul(ps[:, h, 0:HALF], w[:, w_slot, cols], r[:, k, HALF * h:HALF * (h + 1)],
                                       start=(first and n == 0), stop=(last and n == 2))
                return mm

            def unit(u, side, kc, hi, lo, first=False):
                pe.wait_ge(w_lo_ready, u + 1)
                for t in range(2):
                    if not first:
                        pe.wait_ge(tile_read[t], u)
                    for k in range(kc):
                        mm = passes(tiles[t], side, 2 * k + t, hi, lo, k, k == 0, k == kc - 1)
                    mm.then_inc(tile_done[t], 1)

            def unit_by_chunk(u, side, hi, lo, arrive, first=False):
                pe.wait_ge(w_lo_ready, u + 1)
                for t in range(2):
                    if not first:
                        pe.wait_ge(tile_read[t], u)
                for k in range(KD):
                    pe.wait_ge(*arrive(k))
                    for t in range(2):
                        mm = passes(tiles[t], side, 2 * k + t, hi, lo, k, k == 0, k == KD - 1)
                        if k == KD - 1:
                            mm.then_inc(tile_done[t], 1)

            def column_sums(n):
                pe.wait_ge(consts_ready, 1)
                pe.wait_ge(sq_used, KD * (n + 1))
                for h in range(2):
                    mm = pe.matmul(stat_ps[:, h, 0:HALF], ones[:], acc[:, HALF * h:HALF * (h + 1)],
                                   start=True, stop=True)
                mm.then_inc(stat_done, 1)

            def ffn(f, norm, after_first=None, after_up=(), before_up=()):
                for part, n, up, down, before, _ in FFNS[f]:
                    if part:
                        before_up[part]()
                        pairs(pe, n, lambda i, side: unit(up + i, side, KD, hm_hi, hm_lo))
                    else:
                        unit_by_chunk(up, 0, hm_hi, hm_lo, lambda k: (hm_lo_ready, KD * norm + k + 1), first=(up == 0))
                        unit(up + 1, 1, KD, hm_hi, hm_lo)
                        after_first()
                        pairs(pe, n, lambda i, side: unit(up + i, side, KD, hm_hi, hm_lo), first=1)
                    after_up[part]()

                    def down_unit(i, side):
                        pe.wait_ge(h_lo_ready, before + n)
                        unit(down + i, side, n, h_hi, h_lo)
                    pairs(pe, KD // 2, down_unit)

            def nothing():
                pass

            ada_products(0)
            column_sums(0)
            ada_products(1)
            ada_turn(0)
            ada_turn(1)
            ffn(0, 0, after_first=lambda: ada_products(2),
                before_up=(None, lambda: ada_products(3), lambda: ada_products(4)),
                after_up=(lambda: ada_turn(2), lambda: ada_turn(3), lambda: ada_turn(4)))
            ada_products(5)
            column_sums(1)
            unit_by_chunk(GLU, 0, hm_hi, hm_lo, lambda k: (hm_lo_ready, KD + k + 1))
            ada_turn(5)
            unit(GLU + 1, 1, KD, hm_hi, hm_lo)
            pairs(pe, POOL_IN + 2 - GLU, lambda i, side: unit(GLU + i, side, KD, hm_hi, hm_lo), first=1)
            ada_products(6)
            ada_products(7)
            ada_turn(6)
            ada_turn(7)
            pe.wait_ge(wp_lo_ready, 1)
            for g in range(GROUPS):
                pe.wait_ge(pooled_lo_ready, g + 1)
                if g:
                    pe.wait_ge(pmix_hi_ready, g)
                for n, (w, r) in enumerate(((wp_hi, pooled_hi), (wp_hi, pooled_lo), (wp_lo, pooled_hi))):
                    for h in range(2):
                        mm = pe.matmul(stat_ps[:, h, 0:HALF], w[:, g * P:(g + 1) * P],
                                       r[:, g % 2, HALF * h:HALF * (h + 1)], start=(n == 0), stop=(n == 2))
                mm.then_inc(pmix_done, 1)
            pe.wait_ge(pmix_hi_ready, GROUPS)
            for c in range(CONV_CHUNKS):
                pe.wait_ge(conv_tap, 2 * WIDTH * (c + 1))
                for h in range(2):
                    mm = pe.matmul(stat_ps[:, h, 0:HALF], ones[:], v[:, c, HALF * h:HALF * (h + 1)],
                                   start=(c == 0), stop=(c == CONV_CHUNKS - 1))
            mm.then_inc(ln_sum_done, 1)
            pe.wait_ge(mod_ready, 8)
            for c in range(CONV_CHUNKS):
                pe.wait_ge(ln_sq_ready, c + 1)
                for h in range(2):
                    mm = pe.matmul(ada_ps[:, h, 0:HALF], ones[:], sq[:, c % 2, HALF * h:HALF * (h + 1)],
                                   start=(c == 0), stop=(c == CONV_CHUNKS - 1))
                mm.then_inc(ln_var_mm, 1)
            unit_by_chunk(OUT, 0, hm_hi, hm_lo, lambda k: (pmix_lo_ready, k + 1) if k < GROUPS
                          else (vmix_lo_ready, k - GROUPS + 1))
            unit(OUT + 1, 1, KD, hm_hi, hm_lo)
            pairs(pe, KD // 2, lambda i, side: unit(OUT + i, side, KD, hm_hi, hm_lo), first=1)
            ada_products(8)
            column_sums(2)
            ffn(1, 2, after_first=lambda: ada_turn(8), before_up=(None, nothing, nothing),
                after_up=(nothing, nothing, nothing))
            column_sums(3)

        @block.scalar
        def _(act):
            def ada_load(a):
                act.wait_ge(ada_used, a - ADA_SLOTS + 1)
                act.dma_start(ada_raw[:, a % ADA_SLOTS], w_ada[a]).then_inc(ada_raw_ready[a % ADA_SLOTS], 16)

            def ada_load_first(s):
                for q in range(ADA_SLOTS):
                    ada_load(ADA_QUARTERS * s + q)

            def ada_copy(s):
                act.wait_ge(ada_used, ADA_QUARTERS * (s + 1))
                if s:
                    act.wait_ge(ada_turned, s)
                nc.scalar.activation(ada_rows[:], ada_ps[:, s % 2, 0:ADA_N], ACT.Copy).then_inc(ada_copied, 1)

            def split_hi(u, side, first=False):
                act.wait_ge(w_raw_ready[side], 16 * (u // 2 + 1) if isinstance(u, int) else (u - side) * 8 + 16)
                if not first:
                    act.wait_ge(tile_done[1], u - 1)
                nc.scalar.activation(w_hi[:, side, :], w_raw[:, side, :], ACT.Copy).then_inc(w_hi_ready, 1)

            def square(n, c):
                q = KD * n + c
                if n == 0:
                    act.wait_ge(x_in_sem, 16 * KD // 2)
                else:
                    act.wait_ge(x_ready, NORM_TILES[n] - KD + c + 1)
                if q >= 2:
                    act.wait_ge(sq_used, q - 1)
                nc.scalar.activation(sq[:, c % 2, :], x[:, c, :], ACT.Square).then_inc(sq_ready, 1)

            def root(n):
                act.wait_ge(stat_done, n + 1)
                act.wait_ge(consts_ready, 1)
                nc.scalar.activation(by_half(acc[:]), halves(stat_ps), ACT.Sqrt, scale=1.0 / D_MODEL,
                                     bias=eps).then_inc(std_ready, 1)

            def round_hm(n, c):
                act.wait_ge(norm_f, KD * n + c + 1)
                nc.scalar.activation(hm_hi[:, c, :], full[:, c % 2, :], ACT.Copy).then_inc(hm_hi_ready, 1)

            def up_unit(u, side, local, before):
                act.wait_ge(tile_done[0], u + 1)
                nc.scalar.activation(by_half(sil[:]), halves(tile_a), ACT.Silu).then_inc(tile_read[0], 1)
                act.wait_ge(tile_read[1], u + 1)
                nc.scalar.activation(h_hi[:, local, :], full[:, side, :], ACT.Copy).then_inc(h_hi_ready, 1)
                split_hi(u + 2, side)

            def norm(n, next_unit):
                root(n)
                for c in range(KD):
                    round_hm(n, c)
                split_hi(next_unit, next_unit % 2, first=next_unit < 2)

            def ffn(f, norm_after, hooks):
                for part, n, up, down, before, _ in FFNS[f]:
                    if part == 0:
                        first_pair(lambda i, side: up_unit(up + i, side, i, before))
                        hooks[0]()
                        pairs(act, n, lambda i, side: up_unit(up + i, side, i, before), first=1)
                    else:
                        hooks[part]()
                        pairs(act, n, lambda i, side: up_unit(up + i, side, i, before))
                    if part < len(FF_PARTS) - 1:
                        pairs(act, KD // 2, lambda i, side: split_hi(down + i + 2, side))
                    else:
                        for i in range(KD // 2):
                            square(norm_after, 2 * i)
                            square(norm_after, 2 * i + 1)
                            if down + i + 2 < UNITS and i < KD // 2 - 1:
                                split_hi(down + i + 2, i % 2)

            def nothing():
                pass

            act.wait_ge(vec_in, 16)
            act.wait_ge(zeroed, 1)
            nc.scalar.activation(cond[:, :, 0:ROWS], vec[:, V_COND:V_ALL].rearrange("p (k r) -> p k r", r=ROWS),
                                 ACT.Silu).then_inc(cond_ready, 1)
            for c in range(KD):
                square(0, c)
            root(0)
            ada_copy(0)
            ada_copy(1)
            ada_load_first(2)
            split_hi(0, 0, first=True)
            for c in range(KD):
                round_hm(0, c)
            split_hi(1, 1, first=True)

            def ada_next(s, more=True):
                ada_load(ADA_QUARTERS * s + ADA_QUARTERS - 1)
                ada_copy(s)
                if more:
                    ada_load_first(s + 1)

            ffn(0, 1, (lambda: ada_next(2), lambda: ada_next(3), lambda: ada_next(4)))
            ada_load(ADA_QUARTERS * 6 - 1)
            norm(1, GLU + 1)
            ada_copy(5)
            ada_load_first(6)
            act.wait_ge(wp_in, 16)
            act.wait_ge(tile_done[1], GLU)
            nc.scalar.activation(wp_hi[:], wp_raw[:], ACT.Copy).then_inc(wp_hi_ready, 1)
            for c in range(CONV_CHUNKS):
                u = GLU + c
                act.wait_ge(tile_done[0], u + 1)
                if c:
                    act.wait_ge(tile_read[1], u)
                nc.scalar.activation(by_half(sil[:]), halves(tile_a), ACT.Sigmoid).then_inc(tile_read[0], 1)
                split_hi(u + 2, u % 2)
            act.wait_ge(pads_ready, 1)
            act.wait_ge(state_in, 32)
            for g in range(GROUPS):
                u, t = POOL_IN + g // 2, g % 2
                act.wait_ge(tile_done[t], u + 1)
                nc.scalar.activation(split2(pool_p[:, g, POOL_PAD:]), prompt(tiles[t]), ACT.Copy)
                nc.scalar.activation(split2(pool_s[:, g, POOL_PAD * DEC_BATCH:]), sample(tiles[t]),
                                     ACT.Copy).then_inc(tile_read[t], 1)
                if t:
                    split_hi(u + 2, u % 2)
            act.wait_ge(tile_read[0], OUT)
            act.wait_ge(tile_read[1], OUT)
            act.dma_start(conv_p_out, conv_p[:, :, SEQ:]).then_inc(state_out, 16)
            act.dma_start(conv_s_out, conv_s[:, :, DEC_SEQ * DEC_BATCH:]).then_inc(state_out, 16)
            act.dma_start(pool_p_out, pool_p[:, :, SEQ:]).then_inc(state_out, 16)
            act.dma_start(pool_s_out, pool_s[:, :, DEC_SEQ * DEC_BATCH:]).then_inc(state_out, 16)

            def pool_scale(g):
                w = WINDOWS[g]
                act.wait_ge(window_ready, g + 1)
                if g >= 2:
                    act.wait_ge(pooled_lo_ready, g - 1)
                s = sums[:, g % 2, :]
                m = by_half(mean_in[g % 2][:])
                nc.scalar.activation(prompt(m), split2(s[:, POOL_PAD:POOL_P]), ACT.Copy, scale=1.0 / w)
                nc.scalar.activation(sample(m), split2(s[:, POOL_P + POOL_PAD * DEC_BATCH:]), ACT.Copy,
                                     scale=1.0 / w).then_inc(scaled_ready, 1)

            def pool_round(g):
                act.wait_ge(pooled_ready, g + 1)
                if g >= 2:
                    act.wait_ge(pmix_done, g - 1)
                nc.scalar.activation(pooled_hi[:, g % 2, :], mean_in[g % 2][:], ACT.Copy).then_inc(pooled_hi_ready, 1)

            def pmix(g):
                act.wait_ge(pmix_done, g + 1)
                if g >= 2:
                    act.wait_ge(pmix_lo_ready, g - 1)
                nc.scalar.activation(by_half(full[:, g % 2, :]), halves(stat_ps), ACT.Copy, scale=col(V_PSC + g))
                nc.scalar.activation(by_half(hm_hi[:, g, :]), halves(stat_ps), ACT.Copy,
                                     scale=col(V_PSC + g)).then_inc(pmix_hi_ready, 1)

            ada_load(ADA_QUARTERS * 7 - 1)
            pool_scale(0)
            pool_round(0)
            pool_scale(1)
            ada_copy(6)
            ada_load_first(7)
            pool_round(1)
            ada_load(ADA_QUARTERS * 8 - 1)
            pool_scale(2)
            ada_copy(7)
            ada_load_first(8)
            pmix(0)
            pool_round(2)
            pool_scale(3)
            pmix(1)
            pool_round(3)
            pmix(2)
            pmix(3)
            for c in range(CONV_CHUNKS):
                act.wait_ge(ln_centred, c + 1)
                if c >= 2:
                    act.wait_ge(ln_var_mm, c - 1)
                nc.scalar.activation(sq[:, c % 2, :], v[:, c, :], ACT.Square).then_inc(ln_sq_ready, 1)
            act.wait_ge(ln_var_mm, CONV_CHUNKS)
            act.wait_ge(pmix_lo_ready, GROUPS)
            nc.scalar.activation(by_half(acc[:]), halves(ada_ps), ACT.Sqrt, scale=1.0 / D_CONV,
                                 bias=eps).then_inc(ln_std_ready, 1)

            def vmix_buffer(c):
                return (full, sq)[c // 2][:, c % 2, :]

            def vmix_round(c):
                act.wait_ge(vmix_full, c + 1)
                nc.scalar.activation(hm_hi[:, GROUPS + c, :], vmix_buffer(c), ACT.Copy).then_inc(vmix_hi_ready, 1)

            for c in range(CONV_CHUNKS):
                act.wait_ge(ln_scaled, c + 1)
                nc.scalar.activation(vmix_buffer(c), v[:, c, :], ACT.Silu, scale=col(V_LNG + c),
                                     bias=col(V_LNB + c)).then_inc(vmix_full, 1)
                if c:
                    vmix_round(c - 1)
            vmix_round(CONV_CHUNKS - 1)
            for i in range(KD // 2):
                square(2, 2 * i)
                square(2, 2 * i + 1)
                if i < KD // 2 - 1:
                    split_hi(OUT + i + 2, i % 2)
            ada_load(ADA_QUARTERS * 9 - 1)
            norm(2, FFN2 + 1)
            ada_copy(8)
            act.wait_ge(state_out, 16 * 4)
            ffn(1, 3, (nothing, nothing, nothing))
            root(3)

        @block.vector
        def _(dve):
            mod_steps = [0]

            def mod_evacuate(s):
                dve.wait_ge(ada_turned, s + 1)
                dve.wait_ge(vec_in, 16)
                for j in range(2):
                    rows = ada_ps[:, s % 2, ADA_N + P * j:ADA_N + P * (j + 1)].rearrange("p (g r) -> p g r", g=4)[:, :, 0:ROWS]
                    bias = col(V_ADA + KD * s, KD).rearrange("p (g j) -> p g j", j=2)[:, :, j:j + 1]
                    ins = nc.vector.tensor_tensor(
                        mod[:, s].rearrange("p (g j) r -> p g j r", j=2)[:, :, j, :], rows,
                        bias.broadcast_to([P, 4, ROWS]), ALU.add)
                if s not in SCALE and s not in (GATE[0], GATE[2]):
                    ins.then_inc(mod_ready, 1)
                    dve.wait_ge(mod_ready, s + 1)
                    return
                ins.then_inc(mod_step, 1)
                mod_steps[0] += 1
                dve.wait_ge(mod_step, mod_steps[0])
                if s in SCALE:
                    n = SCALE.index(s)
                    g = col(V_G + KD * n, KD).unsqueeze(2).broadcast_to([P, KD, ROWS])
                    nc.vector.scalar_tensor_tensor(gain[:, n], mod[:, s], 1.0, g, ALU.add, ALU.mult).then_inc(mod_ready, 1)
                else:
                    nc.vector.tensor_scalar(mod[:, s], mod[:, s], 0.5, None, ALU.mult).then_inc(mod_ready, 1)
                dve.wait_ge(mod_ready, s + 1)

            def add_square(n, c):
                q = KD * n + c
                dve.wait_ge(sq_ready, q + 1)
                if c == 1:
                    nc.vector.tensor_tensor(acc[:], sq[:, 0, :], sq[:, 1, :], ALU.add).then_inc(sq_used, 2)
                elif c > 1:
                    dve.wait_ge(sq_used, q)
                    nc.vector.tensor_tensor(acc[:], acc[:], sq[:, c % 2, :], ALU.add).then_inc(sq_used, 1)

            def inverse(n):
                dve.wait_ge(std_ready, n + 1)
                nc.vector.reciprocal(rstd[:], acc[:]).then_inc(rstd_ready, 1)
                dve.wait_ge(rstd_ready, n + 1)

            def scale_x(n, c):
                nc.vector.tensor_tensor(sq[:, c % 2, :], x[:, c, :], rstd[:], ALU.mult).then_inc(norm_t, 1)

            def modulate(n, c):
                q = KD * n + c
                t, f = by_half(sq[:, c % 2, :]), by_half(full[:, c % 2, :])
                dve.wait_ge(norm_t, q + 1)
                if c >= 2:
                    dve.wait_ge(hm_lo_ready, q - 1)
                nc.vector.tensor_tensor(steps(sample(f)), steps(sample(t)), over_steps(gain[:, n, c, 1:ROWS]),
                                        ALU.mult).then_inc(norm_fs, 1)
                nc.vector.tensor_scalar(prompt(f), prompt(t), gain[:, n, c, 0:1], mod[:, SHIFT[n], c, 0:1],
                                        ALU.mult, ALU.add)
                dve.wait_ge(norm_fs, q + 1)
                nc.vector.tensor_tensor(steps(sample(f)), steps(sample(f)), over_steps(mod[:, SHIFT[n], c, 1:ROWS]),
                                        ALU.add).then_inc(norm_f, 1)

            def apply_norm(n):
                inverse(n)
                scale_x(n, 0)
                for c in range(KD):
                    if c + 1 < KD:
                        if c >= 1:
                            dve.wait_ge(norm_f, KD * n + c)
                        scale_x(n, c + 1)
                    modulate(n, c)

            def up_unit(u, side, local, before):
                dve.wait_ge(tile_done[1], u + 1)
                dve.wait_ge(tile_read[0], u + 1)
                nc.vector.tensor_tensor(by_half(full[:, side, :]), by_half(sil[:]), halves(tile_b),
                                        ALU.mult).then_inc(tile_read[1], 1)
                dve.wait_ge(h_hi_ready, before + local + 1)
                nc.vector.tensor_tensor(h_lo[:, local, :], full[:, side, :], h_hi[:, local, :].bitcast(F32),
                                        ALU.subtract).then_inc(h_lo_ready, 1)

            def residual(u, m, t, e, s):
                ps = tiles[t]
                xm = by_half(x[:, m, :]) if isinstance(m, int) else by_half(x[:, bass.ds(m, 1), :].rearrange("p o n -> p (o n)"))
                dve.wait_ge(tile_done[t], u + 1)
                g = steps(gated[:, t, :].rearrange("p (h n) -> p h n", h=2))
                nc.vector.tensor_tensor(g, steps(sample(ps)), over_steps(gate_rows(s, m)), ALU.mult).then_inc(gate_tmp, 1)
                nc.vector.scalar_tensor_tensor(prompt(xm), prompt(ps), gate_prompt(s, m), prompt(xm), ALU.mult,
                                               ALU.add).then_inc(tile_read[t], 1)
                dve.wait_ge(gate_tmp, e + 1)
                nc.vector.tensor_tensor(steps(sample(xm)), steps(sample(xm)), g, ALU.add).then_inc(x_ready, 1)

            def gate_rows(s, m):
                return mod[:, s, m, 1:ROWS] if isinstance(m, int) else mod[:, s, bass.ds(m, 1), 1:ROWS].rearrange("p o r -> p (o r)")

            def gate_prompt(s, m):
                return mod[:, s, m, 0:1] if isinstance(m, int) else mod[:, s, bass.ds(m, 1), 0:1].rearrange("p o r -> p (o r)")

            def down_unit(u, i, e0, s):
                for t in range(2):
                    residual(u, i * 2 + t, t, e0 + i * 2 + t, s)

            def down_and_squares(first_unit, e0, s, n):
                for i in range(KD // 2):
                    u = first_unit + i
                    residual(u, 2 * i, 0, e0 + 2 * i, s)
                    if i:
                        add_square(n, 2 * i - 1)
                    residual(u, 2 * i + 1, 1, e0 + 2 * i + 1, s)
                    if i:
                        add_square(n, 2 * i)
                add_square(n, KD - 1)

            def ffn(f, gate, norm_after, hooks):
                for part, n, up, down, before, e0 in FFNS[f]:
                    if part == 0:
                        first_pair(lambda i, side: up_unit(up + i, side, i, before))
                        hooks[0]()
                        pairs(dve, n, lambda i, side: up_unit(up + i, side, i, before), first=1)
                        hooks[1]()
                    else:
                        pairs(dve, n, lambda i, side: up_unit(up + i, side, i, before))
                        hooks[part + 1]()
                    if part < len(FF_PARTS) - 1:
                        pairs(dve, KD // 2, lambda i, side: down_unit(down + i, i, e0, gate))
                    else:
                        down_and_squares(down, e0, gate, norm_after)

            def nothing():
                pass

            for c in range(KD):
                add_square(0, c)
            mod_evacuate(0)
            mod_evacuate(1)
            dve.wait_ge(mod_ready, 2)
            apply_norm(0)
            ffn(0, GATE[0], 1, (nothing, lambda: mod_evacuate(2), lambda: mod_evacuate(3), lambda: mod_evacuate(4)))
            apply_norm(1)

            def glu(c):
                u = GLU + c
                if c == 0:
                    dve.wait_ge(pads_ready, 1)
                    dve.wait_ge(state_in, 32)
                dve.wait_ge(tile_read[0], u + 1)
                dve.wait_ge(tile_done[1], u + 1)
                s = by_half(sil[:])
                nc.vector.tensor_tensor(split2(conv_p[:, c, CONV_PAD:]), prompt(s), prompt(tile_b),
                                        ALU.mult)
                nc.vector.tensor_tensor(split2(conv_s[:, c, CONV_PAD * DEC_BATCH:]), sample(s), sample(tile_b),
                                        ALU.mult).then_inc(tile_read[1], 1)

            def window(c, k):
                if isinstance(k, int):
                    return (split2(conv_p[:, c, k:k + SEQ]),
                            split2(conv_s[:, c, DEC_BATCH * k:DEC_BATCH * (k + DEC_SEQ)]), col(V_WDW + c * WIDTH + k))
                return (split2(conv_p[:, c, bass.ds(k, SEQ)]),
                        split2(conv_s[:, c, bass.ds(k * DEC_BATCH, DEC_BATCH * DEC_SEQ)]),
                        vec[:, bass.ds(k + (V_WDW + c * WIDTH), 1)])

            def conv_start(c):
                vc = by_half(v[:, c, :])
                win_p, win_s, w = window(c, 0)
                dve.wait_ge(tile_read[1], GLU + c + 1)
                nc.vector.tensor_scalar(prompt(vc), win_p, w, col(V_BDW + c), ALU.mult, ALU.add).then_inc(conv_tap, 1)
                nc.vector.tensor_scalar(sample(vc), win_s, w, col(V_BDW + c), ALU.mult, ALU.add).then_inc(conv_tap, 1)

            def conv_taps(c, g0, g1):
                vc = by_half(v[:, c, :])
                with dve.Fori(g0, g1) as g:
                    for kk in range(TAPS_PER_LOOP):
                        k = g * TAPS_PER_LOOP + (kk + 1)
                        done = g * (2 * TAPS_PER_LOOP) + 2 * (kk + 1 + c * WIDTH)
                        win_p, win_s, w = window(c, k)
                        dve.wait_ge(conv_tap, done - 1)
                        nc.vector.scalar_tensor_tensor(prompt(vc), win_p, w, prompt(vc), ALU.mult,
                                                       ALU.add).then_inc(conv_tap, 1)
                        dve.wait_ge(conv_tap, done)
                        nc.vector.scalar_tensor_tensor(sample(vc), win_s, w, sample(vc), ALU.mult,
                                                       ALU.add).then_inc(conv_tap, 1)

            glu(0)
            mod_evacuate(5)
            conv_start(0)
            conv_taps(0, 0, TAP_GROUPS // 2)
            glu(1)
            conv_taps(0, TAP_GROUPS // 2, TAP_GROUPS)
            glu(2)
            conv_start(1)
            conv_taps(1, 0, TAP_GROUPS // 2)
            glu(3)
            conv_taps(1, TAP_GROUPS // 2, TAP_GROUPS)
            conv_start(2)
            conv_taps(2, 0, TAP_GROUPS)
            mod_evacuate(6)
            mod_evacuate(7)
            conv_start(3)
            conv_taps(3, 0, TAP_GROUPS)
            dve.wait_ge(ln_sum_done, 1)
            for c in range(CONV_CHUNKS):
                vc = by_half(v[:, c, :])
                nc.vector.scalar_tensor_tensor(vc, halves(stat_ps), -1.0 / D_CONV, vc, ALU.mult,
                                               ALU.add).then_inc(ln_centred, 1)
            dve.wait_ge(ln_std_ready, 1)
            dve.wait_ge(pmix_lo_ready, GROUPS)
            nc.vector.reciprocal(rstd[:], acc[:]).then_inc(ln_rstd_ready, 1)
            dve.wait_ge(ln_rstd_ready, 1)
            for c in range(CONV_CHUNKS):
                nc.vector.tensor_tensor(v[:, c, :], v[:, c, :], rstd[:], ALU.mult).then_inc(ln_scaled, 1)
            for c in range(CONV_CHUNKS):
                dve.wait_ge(vmix_hi_ready, c + 1)
                nc.vector.tensor_tensor(hm_lo[:, GROUPS + c, :], (full, sq)[c // 2][:, c % 2, :],
                                        hm_hi[:, GROUPS + c, :].bitcast(F32), ALU.subtract).then_inc(vmix_lo_ready, 1)
            dve.wait_ge(mod_ready, 8)
            down_and_squares(OUT, OUT_TILES, GATE[1], 2)
            apply_norm(2)
            ffn(1, GATE[2], 3, (lambda: mod_evacuate(8), nothing, nothing, nothing))
            inverse(3)
            for c in range(KD):
                nc.vector.scalar_tensor_tensor(x[:, c, :], x[:, c, :], col(V_GF + c), rstd[:], ALU.mult,
                                               ALU.mult).then_inc(y_ready, 1)

        @block.gpsimd
        def _(pool):
            def split_lo(u, side):
                pool.wait_ge(w_hi_ready, u + 1)
                nc.gpsimd.tensor_tensor(w_lo[:, side, :], w_raw[:, side, :], w_hi[:, side, :].bitcast(F32),
                                        ALU.subtract).then_inc(w_lo_ready, 1)

            def hm_lows(n):
                for c in range(KD):
                    pool.wait_ge(hm_hi_ready, KD * n + c + 1)
                    nc.gpsimd.tensor_tensor(hm_lo[:, c, :], full[:, c % 2, :], hm_hi[:, c, :].bitcast(F32),
                                            ALU.subtract).then_inc(hm_lo_ready, 1)

            def split_pairs(first, last):
                with pool.Fori(first // 2, last // 2) as i:
                    for side in range(2):
                        split_lo(i * 2 + side, side)

            nc.gpsimd.memset(cond[:], 0.0).then_inc(zeroed, 1)
            nc.gpsimd.memset(ident[:], 0.0).then_inc(ident_zero, 1)
            nc.gpsimd.memset(ones[:], 1.0)
            for t in range(POOL_PAD):
                nc.gpsimd.memset(small[:, t:t + 1], 1.0 / (t + 1))
            nc.gpsimd.memset(eps, EPS).then_inc(consts_ready, 1)
            pool.wait_ge(ident_zero, 1)
            nc.gpsimd.affine_select(out=ident[:], in_=ident[:], compare_op=ALU.not_equal, fill=1.0, base=0,
                                    pattern=[[-1, P]], channel_multiplier=1).then_inc(ident_ready, 1)
            split_lo(0, 0)
            hm_lows(0)
            split_lo(1, 1)
            split_pairs(2, GLU)
            split_lo(GLU, 0)
            hm_lows(1)
            split_lo(GLU + 1, 1)
            pool.wait_ge(tile_done[1], GLU)
            nc.gpsimd.memset(conv_p[:, :, 0:CONV_PAD], 0.0)
            nc.gpsimd.memset(pool_p[:, :, 0:POOL_PAD], 0.0).then_inc(pads_ready, 1)
            for u in range(GLU + 2, GLU + 6):
                split_lo(u, u % 2)
            pool.wait_ge(wp_hi_ready, 1)
            nc.gpsimd.tensor_tensor(wp_lo[:], wp_raw[:], wp_hi[:].bitcast(F32), ALU.subtract).then_inc(wp_lo_ready, 1)

            def window_sums(g):
                pool.wait_ge(tile_read[g % 2], POOL_IN + g // 2 + 1)
                src_p, src_s = pool_p[:, g, :], pool_s[:, g, :]
                for level in range(g + 1):
                    d = 1 << level
                    first = 2 * d - 1
                    dst = sums[:, level % 2, :]
                    dst_p, dst_s = dst[:, 0:POOL_P], dst[:, POOL_P:]
                    if level:
                        pool.wait_ge(pool_step, steps_done[0])
                    nc.gpsimd.tensor_tensor(dst_p[:, first:POOL_P], src_p[:, first:POOL_P],
                                            src_p[:, first - d:POOL_P - d], ALU.add)
                    a, b, n = first * DEC_BATCH, (first - d) * DEC_BATCH, POOL_S - first * DEC_BATCH
                    ins = nc.gpsimd.tensor_tensor(dst_s[:, a:a + n], src_s[:, a:a + n], src_s[:, b:b + n], ALU.add)
                    if level < g:
                        ins.then_inc(pool_step, 1)
                        steps_done[0] += 1
                    else:
                        ins.then_inc(window_ready, 1)
                    src_p, src_s = dst_p, dst_s

            def window_means(g):
                pool.wait_ge(window_ready, g + 1)
                pool.wait_ge(scaled_ready, g + 1)
                m = mean_in[g % 2]
                n = WINDOWS[g] - 1
                nc.gpsimd.tensor_tensor(m[:, 0:n], sums[:, g % 2, POOL_PAD:POOL_PAD + n], small[:, 0:n],
                                        ALU.mult).then_inc(pool_step, 1)
                steps_done[0] += 1
                pool.wait_ge(pool_step, steps_done[0])
                mh = by_half(m[:])
                nc.gpsimd.tensor_tensor(prompt(mh), prompt(mh), split2(pool_p[:, g, POOL_PAD:]), ALU.subtract)
                nc.gpsimd.tensor_tensor(sample(mh), sample(mh), split2(pool_s[:, g, POOL_PAD * DEC_BATCH:]),
                                        ALU.subtract).then_inc(pooled_ready, 1)
                pool.wait_ge(pooled_hi_ready, g + 1)
                nc.gpsimd.tensor_tensor(pooled_lo[:, g % 2, :], m[:], pooled_hi[:, g % 2, :].bitcast(F32),
                                        ALU.subtract).then_inc(pooled_lo_ready, 1)

            steps_done = [0]
            for g in range(GROUPS):
                if g % 2 == 0:
                    split_lo(OUT + g // 2, g // 2)
                window_sums(g)
                window_means(g)
            for g in range(GROUPS):
                pool.wait_ge(pmix_hi_ready, g + 1)
                nc.gpsimd.tensor_tensor(hm_lo[:, g, :], full[:, g % 2, :], hm_hi[:, g, :].bitcast(F32),
                                        ALU.subtract).then_inc(pmix_lo_ready, 1)
            for u in range(OUT + 2, FFN2 + 1):
                split_lo(u, u % 2)
            hm_lows(2)
            split_lo(FFN2 + 1, 1)
            split_pairs(FFN2 + 2, UNITS)


def column_units(w, tiles):
    import numpy as np

    k = w.shape[0] // P
    blocks = w.reshape(k, P, w.shape[1] // P, P)
    out = np.zeros((len(tiles), P, UNIT), w.dtype)
    for n, (a, b) in enumerate(tiles):
        both = np.stack([blocks[:, :, a], blocks[:, :, b]], axis=1)
        out[n, :, :2 * k * P] = both.transpose(2, 0, 1, 3).reshape(P, 2 * k * P)
    return out


def ffn_units(up, down):
    import numpy as np

    n_hidden, first, units = D_FF // P, 0, []
    pairs_out = [(m, m + 1) for m in range(0, KD, 2)]
    for n in FF_PARTS:
        units.append(column_units(up, [(f, n_hidden + f) for f in range(first, first + n)]))
        units.append(column_units(down[first * P:(first + n) * P], pairs_out))
        first += n
    return np.concatenate(units)


def to_halves(xp, xs):
    import numpy as np

    steps = xs.transpose(1, 0, 2).reshape(2, HALF_STEPS * DEC_BATCH, -1)
    both = np.concatenate([xp.reshape(2, HALF_PROMPT, -1), steps], axis=1)
    return both.reshape(TOKENS, -1).T


def chunks(a):
    return a.reshape(a.shape[0] // P, P, *a.shape[1:]).swapaxes(0, 1)


def kernel(**inputs):
    import numpy as np
    import concourse.bacc as bacc
    from concourse.bass_utils import run_bass_kernel_spmd

    a = {k: np.asarray(t) for k, t in inputs.items()}
    pairs_out = [(m, m + 1) for m in range(0, KD, 2)]
    w_in = a["w_in"][0]
    mixed_rows = np.concatenate([a["w_out"][0][D_CONV:], a["w_out"][0][:D_CONV]])
    units = np.concatenate([
        ffn_units(a["w_ffn1_up"][0], a["w_ffn1_down"][0]),
        column_units(w_in, [(CONV_CHUNKS + c, c) for c in range(CONV_CHUNKS)]),
        column_units(w_in, [(2 * CONV_CHUNKS + g, 2 * CONV_CHUNKS + g + 1) for g in range(0, GROUPS, 2)]),
        column_units(mixed_rows, pairs_out),
        ffn_units(a["w_ffn2_up"][0], a["w_ffn2_down"][0])])
    w_ada = a["w_ada"][0].reshape(ADA_QUARTERS, 2, P, N_MOD, D_MODEL).transpose(3, 0, 2, 1, 4)
    w_ada = w_ada.reshape(N_MOD * ADA_QUARTERS, P, 2, D_MODEL)
    cond = np.concatenate([a["c_prompt"], a["c_sample"]])
    vectors = np.concatenate(
        [chunks(a["b_ada"][0])] + [chunks(a[n][0]) for n in ("g_ffn1", "g_mix", "g_ffn2")] + [chunks(a["g_final"])]
        + [chunks(a[n][0]) for n in ("ln_g", "ln_b", "b_dw", "pool_scale")]
        + [chunks(a["w_dw"][0].T).reshape(P, -1), chunks(cond.T).reshape(P, -1)], axis=1)
    arrays = {
        "x_in": chunks(to_halves(a["x_prompt"][0], a["x_sample"])),
        "w_units": units,
        "w_ada": w_ada,
        "w_pool": a["w_pool"][0].transpose(1, 0, 2).reshape(P, GROUPS * P),
        "vectors": vectors,
        "conv_state": chunks(a["state_conv"][0].transpose(2, 1, 0).reshape(D_CONV, -1)),
        "pool_state": chunks(a["state_pool"][0].transpose(2, 1, 0).reshape(D_POOL, -1)),
    }
    arrays = {k: np.ascontiguousarray(t) for k, t in arrays.items()}
    outs = {"y_out": (P, KD, TOKENS), "conv_p_out": (P, CONV_CHUNKS, CONV_PAD), "pool_p_out": (P, GROUPS, POOL_PAD),
            "conv_s_out": (P, CONV_CHUNKS, CONV_PAD * DEC_BATCH), "pool_s_out": (P, GROUPS, POOL_PAD * DEC_BATCH)}
    nc = bacc.Bacc("TRN2", target_bir_lowering=False, num_devices=1)
    args = [nc.dram_tensor(k, t.shape, mybir.dt.from_np(t.dtype), kind="ExternalInput").ap() for k, t in arrays.items()]
    args += [nc.dram_tensor(k, s, F32, kind="ExternalOutput").ap() for k, s in outs.items()]
    trunk(nc, *args)
    got = run_bass_kernel_spmd(nc, [arrays], core_ids=[0]).results[0]

    def rows(name):
        t = np.asarray(got[name])
        return t.transpose(2, 1, 0).reshape(t.shape[2], -1)

    y = rows("y_out").reshape(2, HALF, D_MODEL)
    y_sample = y[:, HALF_PROMPT:].reshape(DEC_SEQ, DEC_BATCH, D_MODEL).swapaxes(0, 1)
    return (np.ascontiguousarray(y[:, :HALF_PROMPT].reshape(1, SEQ, D_MODEL)),
            np.ascontiguousarray(y_sample),
            np.ascontiguousarray(rows("conv_p_out")[None, None]),
            np.ascontiguousarray(rows("pool_p_out")[None, None]),
            np.ascontiguousarray(rows("conv_s_out").reshape(CONV_PAD, DEC_BATCH, D_CONV).swapaxes(0, 1)[None]),
            np.ascontiguousarray(rows("pool_s_out").reshape(POOL_PAD, DEC_BATCH, D_POOL).swapaxes(0, 1)[None]))
```

```python
from contextlib import ExitStack

import concourse.bass as bass
from concourse import mybir

F32 = mybir.dt.float32
F32R = mybir.dt.float32r
ALU = mybir.AluOpType
ACT = mybir.ActivationFunctionType

P = 128
D_MODEL = 1024
SEQ = 512
DEC_BATCH = 8
DEC_SEQ = 8
D_CONV = 512
D_POOL = 512
WIDTH = 31
WINDOWS = (2, 4, 8, 16)
POOL_MAX = max(WINDOWS)
D_FF = 2816
N_MOD = 9
EPS = 1e-6

KD = D_MODEL // P
CONV_CHUNKS = D_CONV // P
GROUPS = len(WINDOWS)
ROWS = 1 + DEC_BATCH
TOKENS = SEQ + DEC_SEQ * DEC_BATCH
HALF = TOKENS // 2
HALF_PROMPT = SEQ // 2
HALF_STEPS = DEC_SEQ // 2

TOKEN_BLOCKS = -(-TOKENS // P)

UNIT = 16 * P
FF_PARTS = (8, 8, 6)
FFN_UNITS = sum(FF_PARTS) + len(FF_PARTS) * KD // 2
FFN1 = 0
GLU = FFN1 + FFN_UNITS
POOL_IN = GLU + CONV_CHUNKS
OUT = POOL_IN + GROUPS // 2
FFN2 = OUT + KD // 2
UNITS = FFN2 + FFN_UNITS

CONV_PAD = WIDTH - 1
POOL_PAD = POOL_MAX - 1
CONV_P = CONV_PAD + SEQ
CONV_S = (CONV_PAD + DEC_SEQ) * DEC_BATCH
POOL_P = POOL_PAD + SEQ
POOL_S = (POOL_PAD + DEC_SEQ) * DEC_BATCH
TAPS_PER_LOOP = 5
TAP_GROUPS = (WIDTH - 1) // TAPS_PER_LOOP

ADA_SLOTS = 3
ADA_QUARTERS = 4
ADA_N = D_MODEL // 4
SHIFT = (0, 3, 6)
SCALE = (1, 4, 7)
GATE = (2, 5, 8)

V_ADA, V_G, V_GF = 0, 72, 96
V_LNG, V_LNB, V_BDW, V_PSC = 104, 108, 112, 116
V_WDW = 120
V_COND = V_WDW + CONV_CHUNKS * WIDTH
V_ALL = V_COND + KD * ROWS


def trunk(nc, x_in, w_units, w_ada, w_pool, vectors, conv_state, pool_state,
          y_out, conv_p_out, pool_p_out, conv_s_out, pool_s_out):
    ctx = ExitStack()
    with ctx:
        def sb(name, shape, dt=F32):
            return ctx.enter_context(nc.sbuf_tensor(name, shape, dt))

        def sem(name):
            return ctx.enter_context(nc.semaphore(name))

        with nc.sbuf_tensor("h_hi", [P, 8, TOKENS], F32R) as h_hi, \
                nc.sbuf_tensor("h_lo", [P, 8, TOKENS], F32R) as h_lo:
            pass
        with ExitStack() as under:
            def alias(name, shape, dt=F32):
                return under.enter_context(nc.sbuf_tensor(name, shape, dt))
            conv_p = alias("conv_p", [P, CONV_CHUNKS, CONV_P])
            v = alias("v", [P, CONV_CHUNKS, TOKENS])
            pool_p = alias("pool_p", [P, GROUPS, POOL_P])
            sums = alias("sums", [P, 2, POOL_P + POOL_S])
            wp_hi = alias("wp_hi", [P, GROUPS * P], F32R)
            wp_lo = alias("wp_lo", [P, GROUPS * P], F32R)
        ctx.enter_context(nc.sbuf_tensor("h_room", [P, 2 * 8 * TOKENS], F32))

        x = sb("x", [P, KD, TOKENS])
        hm_hi = sb("hm_hi", [P, KD, TOKENS], F32R)
        hm_lo = sb("hm_lo", [P, KD, TOKENS], F32R)
        w_raw = sb("w_raw", [P, 2, UNIT])
        w_hi = sb("w_hi", [P, 2, UNIT], F32R)
        w_lo = sb("w_lo", [P, 2, UNIT], F32R)
        ada_raw = sb("ada_raw", [P, ADA_SLOTS, 2, D_MODEL])
        vec = sb("vec", [P, V_ALL])
        cond = sb("cond", [P, KD, 32])
        ident = sb("ident", [P, P])
        ones = sb("ones", [P, P])
        small = sb("small", [P, POOL_PAD + 2])
        rms = sb("rms", [P, 2, TOKEN_BLOCKS])
        ada_rows = sb("ada_rows", [P, ADA_N])
        mod = sb("mod", [P, N_MOD, KD, ROWS])
        gain = sb("gain", [P, 3, KD, ROWS])
        sil = sb("sil", [P, TOKENS])
        full = sb("full", [P, 2, TOKENS])
        sq = sb("sq", [P, 2, TOKENS])
        acc = sb("acc", [P, TOKENS])
        rstd = sb("rstd", [P, TOKENS])
        gated = sb("gated", [P, 2, HALF_STEPS * DEC_BATCH * 2])
        conv_s = sb("conv_s", [P, CONV_CHUNKS, CONV_S])
        pool_s = sb("pool_s", [P, GROUPS, POOL_S])
        wp_raw = sb("wp_raw", [P, GROUPS * P])
        pooled_hi = sb("pooled_hi", [P, 2, TOKENS], F32R)
        pooled_lo = sb("pooled_lo", [P, 2, TOKENS], F32R)
        mean_in = [acc, rstd]
        eps, scrap = small[:, POOL_PAD:POOL_PAD + 1], small[:, POOL_PAD + 1:POOL_PAD + 2]

        def bank2(name):
            return ctx.enter_context(nc.psum_tensor(name, [P, 2, 512], F32))
        tile_a, tile_b, stat_ps, ada_ps = (bank2(n) for n in ("tile_a", "tile_b", "stat_ps", "ada_ps"))
        tiles = (tile_a, tile_b)
        r_ps = stat_ps.rearrange("p h n -> p (h n)")[:, 0:TOKENS]
        sums_ps = stat_ps[:, 1, 512 - TOKEN_BLOCKS:512]

        vec_in, x_in_sem, state_in, wp_in = sem("vec_in"), sem("x_in_sem"), sem("state_in"), sem("wp_in")
        w_raw_ready = [sem("w_raw_ready0"), sem("w_raw_ready1")]
        ada_raw_ready = [sem(f"ada_raw_ready{n}") for n in range(ADA_SLOTS)]
        state_out, y_sent = sem("state_out"), sem("y_sent")
        zeroed, ident_zero, ident_ready, consts_ready, cond_ready = (
            sem("zeroed"), sem("ident_zero"), sem("ident_ready"), sem("consts_ready"), sem("cond_ready"))
        ada_used, ada_copied, ada_turned = sem("ada_used"), sem("ada_copied"), sem("ada_turned")
        mod_step, mod_ready = sem("mod_step"), sem("mod_ready")
        w_hi_ready, w_lo_ready = sem("w_hi_ready"), sem("w_lo_ready")
        tile_done = (sem("tile_a_done"), sem("tile_b_done"))
        tile_read = (sem("tile_a_read"), sem("tile_b_read"))
        h_hi_ready, h_lo_ready = sem("h_hi_ready"), sem("h_lo_ready")
        gate_tmp, x_ready = sem("gate_tmp"), sem("x_ready")
        sq_ready, sq_used, stat_done, std_ready, rstd_ready = (
            sem("sq_ready"), sem("sq_used"), sem("stat_done"), sem("std_ready"), sem("rstd_ready"))
        r_ready, norm_s1, norm_s2 = sem("r_ready"), sem("norm_s1"), sem("norm_s2")
        norm_t, norm_fs, norm_f = sem("norm_t"), sem("norm_fs"), sem("norm_f")
        hm_hi_ready, y_ready = sem("hm_hi_ready"), sem("y_ready")
        hm_lo_ready = (sem("hm_lo_even_ready"), sem("hm_lo_odd_ready"))
        pads_ready, conv_tap = sem("pads_ready"), sem("conv_tap")
        pool_in_ready, pool_step, window_ready, scaled_ready, pooled_ready = (
            sem("pool_in_ready"), sem("pool_step"), sem("window_ready"), sem("scaled_ready"), sem("pooled_ready"))
        wp_hi_ready, wp_lo_ready = sem("wp_hi_ready"), sem("wp_lo_ready")
        pooled_hi_ready, pooled_lo_ready = sem("pooled_hi_ready"), sem("pooled_lo_ready")
        pmix_done, pmix_hi_ready, pmix_lo_ready = sem("pmix_done"), sem("pmix_hi_ready"), sem("pmix_lo_ready")
        ln_sum_done, ln_centred, ln_sq_ready, ln_var_mm = (
            sem("ln_sum_done"), sem("ln_centred"), sem("ln_sq_ready"), sem("ln_var_mm"))
        ln_std_ready, ln_rstd_ready, ln_scaled = sem("ln_std_ready"), sem("ln_rstd_ready"), sem("ln_scaled")
        vmix_full, vmix_hi_ready, vmix_lo_ready = sem("vmix_full"), sem("vmix_hi_ready"), sem("vmix_lo_ready")

        def halves(ps):
            return ps[:, :, 0:HALF]

        def by_half(t):
            return t.rearrange("p (h n) -> p h n", h=2)

        def prompt(t):
            return t[:, :, 0:HALF_PROMPT]

        def sample(t):
            return t[:, :, HALF_PROMPT:HALF]

        def steps(t):
            return t.rearrange("p h (t b) -> p h t b", b=DEC_BATCH)

        def over_steps(rows):
            return rows.unsqueeze(1).unsqueeze(1).broadcast_to([P, 2, HALF_STEPS, DEC_BATCH])

        def split2(t):
            return t.rearrange("p (h n) -> p h n", h=2)

        def col(a, n=1):
            return vec[:, a:a + n]

        def ffn_parts(first_unit, ffn):
            u, out = first_unit, []
            for part, n in enumerate(FF_PARTS):
                before = ffn * sum(FF_PARTS) + sum(FF_PARTS[:part])
                tiles_before = ffn * (len(FF_PARTS) + 1) * KD + part * KD
                out.append((part, n, u, u + n, before, tiles_before))
                u += n + KD // 2
            return out

        FFNS = (ffn_parts(FFN1, 0), ffn_parts(FFN2, 1))
        OUT_TILES = len(FF_PARTS) * KD
        NORM_TILES = (0, OUT_TILES, OUT_TILES + KD, 2 * OUT_TILES + KD)

        def pairs(eng, count, body, first=0):
            if count // 2 - first == 1:
                for side in range(2):
                    body(2 * first + side, side)
            elif count // 2 > first:
                with eng.Fori(first, count // 2) as i:
                    for side in range(2):
                        body(i * 2 + side, side)

        def pairs_and(eng, count, body, between, first=0):
            for stop in sorted(set(between) | {count // 2}):
                pairs(eng, 2 * stop, body, first)
                first = max(first, stop)
                if stop in between:
                    between[stop]()

        def lo_at(n, c):
            return hm_lo_ready[c % 2], KD // 2 * n + c // 2 + 1

        block = ctx.enter_context(nc.Block())

        @block.sync
        def _(sp):
            sp.dma_start(vec[:], vectors).then_inc(vec_in, 16)
            for c in range(0, KD, 2):
                sp.dma_start(x[:, c:c + 2, :], x_in[:, c:c + 2, :]).then_inc(x_in_sem, 16)
            for a in range(2 * ADA_QUARTERS):
                if a >= ADA_SLOTS:
                    sp.wait_ge(ada_used, a - ADA_SLOTS + 1)
                sp.dma_start(ada_raw[:, a % ADA_SLOTS], w_ada[a]).then_inc(ada_raw_ready[a % ADA_SLOTS], 16)
            for u in range(2):
                sp.dma_start(w_raw[:, u, :], w_units[u]).then_inc(w_raw_ready[u], 16)
            sp.dma_start(conv_s[:, :, 0:CONV_PAD * DEC_BATCH], conv_state).then_inc(state_in, 16)
            sp.dma_start(pool_s[:, :, 0:POOL_PAD * DEC_BATCH], pool_state).then_inc(state_in, 16)
            sp.dma_start(wp_raw[:], w_pool).then_inc(wp_in, 16)
            with sp.Fori(1, UNITS // 2) as i:
                for side in range(2):
                    sp.wait_ge(w_lo_ready, i * 2 + (side - 1))
                    sp.dma_start(w_raw[:, side, :], w_units[i * 2 + side]).then_inc(w_raw_ready[side], 16)
            for c in range(KD):
                sp.wait_ge(y_ready, c + 1)
                sp.dma_start(y_out[:, c, :], x[:, c, :]).then_inc(y_sent, 16)
            sp.wait_ge(y_sent, 16 * KD)
            sp.wait_ge(state_out, 16 * 4)

        @block.tensor
        def _(pe):
            def ada_products(s, first=0, last=ADA_QUARTERS):
                pe.wait_ge(cond_ready, 1)
                if s >= 2 and first == 0:
                    pe.wait_ge(ada_copied, s - 1)
                for q in range(first, last):
                    a = ADA_QUARTERS * s + q
                    pe.wait_ge(ada_raw_ready[a % ADA_SLOTS], 16 * (a // ADA_SLOTS + 1))
                    for kk in range(2):
                        k = 2 * q + kk
                        for g in range(4):
                            mm = pe.matmul(ada_ps[32 * g:32 * g + 32, s % 2, 0:ADA_N], cond[:, k, :],
                                           ada_raw[:, a % ADA_SLOTS, kk, ADA_N * g:ADA_N * (g + 1)],
                                           start=(k == 0), stop=(k == KD - 1))
                    mm.then_inc(ada_used, 1)

            def ada_turn(s):
                pe.wait_ge(ada_copied, s + 1)
                pe.wait_ge(ident_ready, 1)
                if s >= 2:
                    pe.wait_ge(mod_ready, s - 1)
                for j in range(2):
                    mm = pe.transpose(ada_ps[:, s % 2, ADA_N + P * j:ADA_N + P * (j + 1)],
                                      ada_rows[:, P * j:P * (j + 1)], ident[:])
                mm.then_inc(ada_turned, 1)

            def passes(ps, w_slot, block_col, hi, lo, k, first, last):
                cols = slice(block_col * P, (block_col + 1) * P)
                for n, (w, r) in enumerate(((w_hi, hi), (w_hi, lo), (w_lo, hi))):
                    for h in range(2):
                        mm = pe.matmul(ps[:, h, 0:HALF], w[:, w_slot, cols], r[:, k, HALF * h:HALF * (h + 1)],
                                       start=(first and n == 0), stop=(last and n == 2))
                return mm

            def unit(u, side, kc, hi, lo, hidden=None):
                pe.wait_ge(w_lo_ready, u + 1)
                if hidden is not None:
                    pe.wait_ge(h_lo_ready, hidden - 1)
                for t in range(2):
                    pe.wait_ge(tile_read[t], u)
                    for k in range(kc):
                        if hidden is not None and t == 0 and k == kc - 1:
                            pe.wait_ge(h_lo_ready, hidden)
                        mm = passes(tiles[t], side, 2 * k + t, hi, lo, k, k == 0, k == kc - 1)
                    mm.then_inc(tile_done[t], 1)

            def unit_by_chunk(u, side, hi, lo, arrive, first=False):
                pe.wait_ge(w_lo_ready, u + 1)
                for t in range(2):
                    if not first:
                        pe.wait_ge(tile_read[t], u)
                for k in range(KD):
                    pe.wait_ge(*arrive(k))
                    for t in range(2):
                        mm = passes(tiles[t], side, 2 * k + t, hi, lo, k, k == 0, k == KD - 1)
                        if k == KD - 1:
                            mm.then_inc(tile_done[t], 1)

            def column_sums(n):
                pe.wait_ge(consts_ready, 1)
                pe.wait_ge(sq_used, (KD - 1) * (n + 1))
                pe.wait_ge(sq_ready, KD * (n + 1))
                token_sums([acc[:], sq[:, 1, :]]).then_inc(stat_done, 1)

            def token_sums(parts):
                for j in range(TOKEN_BLOCKS):
                    first = min(P * j, TOKENS - P)
                    for n, part in enumerate(parts):
                        mm = pe.matmul(sums_ps[:, j:j + 1], part[:, first:first + P], ones[:, 0:1],
                                       start=(n == 0), stop=(n == len(parts) - 1))
                return mm

            def spread(n):
                pe.wait_ge(ident_ready, 1)
                pe.wait_ge(rstd_ready, n + 1)
                for j in range(TOKEN_BLOCKS):
                    first = max(0, P * (j + 1) - TOKENS)
                    mm = pe.transpose(r_ps[:, P * j:P * (j + 1) - first],
                                      rms[first:, 1, j:j + 1].broadcast_to([P - first, P]), ident[first:, first:])
                mm.then_inc(r_ready, 1)

            def ffn(f, norm, between):
                for part, n, up, down, before, _ in FFNS[f]:
                    if part == 0:
                        unit_by_chunk(up, 0, hm_hi, hm_lo, lambda k: lo_at(norm, k), first=(up == 0))
                        unit(up + 1, 1, KD, hm_hi, hm_lo)
                    pairs_and(pe, n, lambda i, side: unit(up + i, side, KD, hm_hi, hm_lo), between[part],
                              first=(part == 0))
                    pairs(pe, KD // 2, lambda i, side: unit(down + i, side, n, h_hi, h_lo, hidden=before + n))

            ada_products(0)
            column_sums(0)
            ada_products(1)
            spread(0)
            ada_turn(0)
            ada_turn(1)
            ffn(0, 0, ({1: lambda: ada_products(2, 0, 3), 2: lambda: ada_products(2, 3), 4: lambda: ada_turn(2)},
                       {0: lambda: ada_products(3, 0, 3), 1: lambda: ada_products(3, 3), 4: lambda: ada_turn(3)},
                       {0: lambda: ada_products(4, 0, 3), 1: lambda: ada_products(4, 3), 3: lambda: ada_turn(4)}))
            ada_products(5, 0, 2)
            column_sums(1)
            ada_products(5, 2, 3)
            spread(1)
            ada_products(5, 3)
            unit_by_chunk(GLU, 0, hm_hi, hm_lo, lambda k: lo_at(1, k))
            ada_turn(5)
            unit(GLU + 1, 1, KD, hm_hi, hm_lo)
            pairs(pe, POOL_IN + 2 - GLU, lambda i, side: unit(GLU + i, side, KD, hm_hi, hm_lo), first=1)
            ada_products(6)
            ada_products(7)
            ada_turn(6)
            ada_turn(7)
            pe.wait_ge(wp_lo_ready, 1)
            for g in range(GROUPS):
                pe.wait_ge(pooled_lo_ready, g + 1)
                if g:
                    pe.wait_ge(pmix_hi_ready, g)
                for n, (w, r) in enumerate(((wp_hi, pooled_hi), (wp_hi, pooled_lo), (wp_lo, pooled_hi))):
                    for h in range(2):
                        mm = pe.matmul(stat_ps[:, h, 0:HALF], w[:, g * P:(g + 1) * P],
                                       r[:, g % 2, HALF * h:HALF * (h + 1)], start=(n == 0), stop=(n == 2))
                mm.then_inc(pmix_done, 1)
            pe.wait_ge(pmix_hi_ready, GROUPS)
            for c in range(CONV_CHUNKS):
                pe.wait_ge(conv_tap, 2 * WIDTH * (c + 1))
                for h in range(2):
                    mm = pe.matmul(stat_ps[:, h, 0:HALF], ones[:], v[:, c, HALF * h:HALF * (h + 1)],
                                   start=(c == 0), stop=(c == CONV_CHUNKS - 1))
            mm.then_inc(ln_sum_done, 1)
            pe.wait_ge(mod_ready, 8)
            for c in range(CONV_CHUNKS):
                pe.wait_ge(ln_sq_ready, c + 1)
                for h in range(2):
                    mm = pe.matmul(ada_ps[:, h, 0:HALF], ones[:], sq[:, c % 2, HALF * h:HALF * (h + 1)],
                                   start=(c == 0), stop=(c == CONV_CHUNKS - 1))
                mm.then_inc(ln_var_mm, 1)
            unit_by_chunk(OUT, 0, hm_hi, hm_lo, lambda k: (pmix_lo_ready, k + 1) if k < GROUPS
                          else (vmix_lo_ready, k - GROUPS + 1))
            unit(OUT + 1, 1, KD, hm_hi, hm_lo)
            pairs(pe, KD // 2, lambda i, side: unit(OUT + i, side, KD, hm_hi, hm_lo), first=1)
            ada_products(8, 0, 2)
            column_sums(2)
            ada_products(8, 2, 3)
            spread(2)
            ada_products(8, 3)
            ffn(1, 2, ({1: lambda: ada_turn(8)}, {}, {}))
            column_sums(3)
            spread(3)

        @block.scalar
        def _(act):
            def ada_load(a):
                act.wait_ge(ada_used, a - ADA_SLOTS + 1)
                act.dma_start(ada_raw[:, a % ADA_SLOTS], w_ada[a]).then_inc(ada_raw_ready[a % ADA_SLOTS], 16)

            def ada_load_first(s):
                for q in range(ADA_SLOTS):
                    ada_load(ADA_QUARTERS * s + q)

            def ada_copy(s):
                act.wait_ge(ada_used, ADA_QUARTERS * (s + 1))
                if s:
                    act.wait_ge(ada_turned, s)
                nc.scalar.activation(ada_rows[:], ada_ps[:, s % 2, 0:ADA_N], ACT.Copy).then_inc(ada_copied, 1)

            def split_hi(u, side, first=False):
                act.wait_ge(w_raw_ready[side], 16 * (u // 2 + 1) if isinstance(u, int) else (u - side) * 8 + 16)
                if not first:
                    act.wait_ge(tile_done[1], u - 1)
                nc.scalar.activation(w_hi[:, side, :], w_raw[:, side, :], ACT.Copy).then_inc(w_hi_ready, 1)

            def square(n, c):
                if n == 0:
                    act.wait_ge(x_in_sem, 16 * KD // 2)
                else:
                    act.wait_ge(x_ready, NORM_TILES[n] - KD + c + 1)
                if c >= 2:
                    act.wait_ge(sq_used, (KD - 1) * n + c - 1)
                nc.scalar.activation(sq[:, c % 2, :], x[:, c, :], ACT.Square).then_inc(sq_ready, 1)

            def load_table(function):
                act.wait_ge(consts_ready, 1)
                nc.scalar.activation(scrap, eps, function)

            def root(n):
                act.wait_ge(stat_done, n + 1)
                nc.scalar.activation(rms[:, 0, :], sums_ps, ACT.Sqrt, scale=1.0 / D_MODEL,
                                     bias=eps).then_inc(std_ready, 1)

            def round_hm(n, c):
                q = KD * n + c
                act.wait_ge(norm_t, q + 1)
                if c >= 2:
                    act.wait_ge(*lo_at(n, c - 2))
                nc.scalar.activation(prompt(by_half(full[:, c % 2, :])), prompt(by_half(sq[:, c % 2, :])),
                                     ACT.Identity, bias=mod[:, SHIFT[n], c, 0:1]).then_inc(norm_f, 1)
                act.wait_ge(norm_f, q + 1)
                act.wait_ge(norm_fs, q + 1)
                nc.scalar.activation(hm_hi[:, c, :], full[:, c % 2, :], ACT.Copy).then_inc(hm_hi_ready, 1)

            def up_unit(u, side, local, before):
                act.wait_ge(tile_done[0], u + 1)
                nc.scalar.activation(by_half(sil[:]), halves(tile_a), ACT.Silu).then_inc(tile_read[0], 1)
                act.wait_ge(tile_read[1], u + 1)
                nc.scalar.activation(h_hi[:, local, :], full[:, side, :], ACT.Copy).then_inc(h_hi_ready, 1)
                split_hi(u + 2, side)

            def norm(n, next_unit):
                root(n)
                split_hi(next_unit, next_unit % 2, first=next_unit < 2)
                load_table(ACT.Silu if n != 1 else ACT.Sigmoid)
                for c in range(KD):
                    round_hm(n, c)

            def ffn(f, norm_after, between):
                for part, n, up, down, before, _ in FFNS[f]:
                    pairs_and(act, n, lambda i, side: up_unit(up + i, side, i, before), between[part])
                    if part < len(FF_PARTS) - 1:
                        pairs(act, KD // 2, lambda i, side: split_hi(down + i + 2, side))
                    else:
                        squares(norm_after, down)

            def squares(n, first_unit):
                for i in range(KD // 2):
                    if i == KD // 2 - 1:
                        load_table(ACT.Sqrt)
                    square(n, 2 * i)
                    square(n, 2 * i + 1)
                    if first_unit + i + 2 < UNITS and i < KD // 2 - 1:
                        split_hi(first_unit + i + 2, i % 2)

            def ada_last_quarter(s):
                ada_load(ADA_QUARTERS * s + ADA_QUARTERS - 1)

            act.wait_ge(vec_in, 16)
            act.wait_ge(zeroed, 1)
            nc.scalar.activation(cond[:, :, 0:ROWS], vec[:, V_COND:V_ALL].rearrange("p (k r) -> p k r", r=ROWS),
                                 ACT.Silu).then_inc(cond_ready, 1)
            for c in range(KD):
                square(0, c)
            root(0)
            ada_copy(0)
            ada_copy(1)
            ada_load_first(2)
            split_hi(0, 0, first=True)
            load_table(ACT.Silu)
            for c in range(KD):
                round_hm(0, c)
            split_hi(1, 1, first=True)

            def ada_next(s):
                ada_copy(s)
                ada_load_first(s + 1)

            ffn(0, 1, ({1: lambda: ada_last_quarter(2), 2: lambda: ada_next(2)},
                       {1: lambda: ada_last_quarter(3), 2: lambda: ada_next(3)},
                       {1: lambda: ada_last_quarter(4), 2: lambda: ada_next(4)}))
            ada_last_quarter(5)
            norm(1, GLU + 1)
            ada_copy(5)
            ada_load_first(6)
            act.wait_ge(wp_in, 16)
            act.wait_ge(tile_done[1], GLU)
            nc.scalar.activation(wp_hi[:], wp_raw[:], ACT.Copy).then_inc(wp_hi_ready, 1)
            for c in range(CONV_CHUNKS):
                u = GLU + c
                act.wait_ge(tile_done[0], u + 1)
                if c:
                    act.wait_ge(tile_read[1], u)
                nc.scalar.activation(by_half(sil[:]), halves(tile_a), ACT.Sigmoid).then_inc(tile_read[0], 1)
                split_hi(u + 2, u % 2)
            act.wait_ge(pads_ready, 1)
            act.wait_ge(state_in, 32)
            for g in range(GROUPS):
                u, t = POOL_IN + g // 2, g % 2
                act.wait_ge(tile_done[t], u + 1)
                nc.scalar.activation(split2(pool_p[:, g, POOL_PAD:]), prompt(tiles[t]), ACT.Copy)
                nc.scalar.activation(split2(pool_s[:, g, POOL_PAD * DEC_BATCH:]), sample(tiles[t]),
                                     ACT.Copy).then_inc(tile_read[t], 1)
                if t:
                    split_hi(u + 2, u % 2)
            act.wait_ge(tile_read[0], OUT)
            act.wait_ge(tile_read[1], OUT)
            act.dma_start(conv_p_out, conv_p[:, :, SEQ:]).then_inc(state_out, 16)
            act.dma_start(conv_s_out, conv_s[:, :, DEC_SEQ * DEC_BATCH:]).then_inc(state_out, 16)
            act.dma_start(pool_p_out, pool_p[:, :, SEQ:]).then_inc(state_out, 16)
            act.dma_start(pool_s_out, pool_s[:, :, DEC_SEQ * DEC_BATCH:]).then_inc(state_out, 16)

            def pool_scale(g):
                w = WINDOWS[g]
                act.wait_ge(window_ready, g + 1)
                if g >= 2:
                    act.wait_ge(pooled_lo_ready, g - 1)
                s = sums[:, g % 2, :]
                m = by_half(mean_in[g % 2][:])
                nc.scalar.activation(prompt(m), split2(s[:, POOL_PAD:POOL_P]), ACT.Copy, scale=1.0 / w)
                nc.scalar.activation(sample(m), split2(s[:, POOL_P + POOL_PAD * DEC_BATCH:]), ACT.Copy,
                                     scale=1.0 / w).then_inc(scaled_ready, 1)

            def pool_round(g):
                act.wait_ge(pooled_ready, g + 1)
                if g >= 2:
                    act.wait_ge(pmix_done, g - 1)
                nc.scalar.activation(pooled_hi[:, g % 2, :], mean_in[g % 2][:], ACT.Copy).then_inc(pooled_hi_ready, 1)

            def pmix(g):
                act.wait_ge(pmix_done, g + 1)
                if g >= 2:
                    act.wait_ge(pmix_lo_ready, g - 1)
                nc.scalar.activation(by_half(full[:, g % 2, :]), halves(stat_ps), ACT.Copy, scale=col(V_PSC + g))
                nc.scalar.activation(by_half(hm_hi[:, g, :]), halves(stat_ps), ACT.Copy,
                                     scale=col(V_PSC + g)).then_inc(pmix_hi_ready, 1)

            ada_load(ADA_QUARTERS * 7 - 1)
            pool_scale(0)
            pool_round(0)
            pool_scale(1)
            ada_copy(6)
            ada_load_first(7)
            pool_round(1)
            ada_load(ADA_QUARTERS * 8 - 1)
            pool_scale(2)
            ada_copy(7)
            ada_load_first(8)
            pmix(0)
            pool_round(2)
            pool_scale(3)
            pmix(1)
            pool_round(3)
            pmix(2)
            pmix(3)
            for c in range(CONV_CHUNKS):
                act.wait_ge(ln_centred, c + 1)
                if c >= 2:
                    act.wait_ge(ln_var_mm, c - 1)
                nc.scalar.activation(sq[:, c % 2, :], v[:, c, :], ACT.Square).then_inc(ln_sq_ready, 1)
            act.wait_ge(ln_var_mm, CONV_CHUNKS)
            act.wait_ge(pmix_lo_ready, GROUPS)
            nc.scalar.activation(by_half(acc[:]), halves(ada_ps), ACT.Sqrt, scale=1.0 / D_CONV,
                                 bias=eps).then_inc(ln_std_ready, 1)

            def vmix_buffer(c):
                return (full, sq)[c // 2][:, c % 2, :]

            def vmix_round(c):
                act.wait_ge(vmix_full, c + 1)
                nc.scalar.activation(hm_hi[:, GROUPS + c, :], vmix_buffer(c), ACT.Copy).then_inc(vmix_hi_ready, 1)

            for c in range(CONV_CHUNKS):
                act.wait_ge(ln_scaled, c + 1)
                nc.scalar.activation(vmix_buffer(c), v[:, c, :], ACT.Silu, scale=col(V_LNG + c),
                                     bias=col(V_LNB + c)).then_inc(vmix_full, 1)
                if c:
                    vmix_round(c - 1)
            vmix_round(CONV_CHUNKS - 1)
            squares(2, OUT)
            ada_last_quarter(8)
            norm(2, FFN2 + 1)
            ada_copy(8)
            act.wait_ge(state_out, 16 * 4)
            ffn(1, 3, ({}, {}, {}))
            root(3)

        @block.vector
        def _(dve):
            mod_steps = [0]

            def mod_evacuate(s):
                dve.wait_ge(ada_turned, s + 1)
                dve.wait_ge(vec_in, 16)
                for j in range(2):
                    rows = ada_ps[:, s % 2, ADA_N + P * j:ADA_N + P * (j + 1)].rearrange("p (g r) -> p g r", g=4)[:, :, 0:ROWS]
                    bias = col(V_ADA + KD * s, KD).rearrange("p (g j) -> p g j", j=2)[:, :, j:j + 1]
                    ins = nc.vector.tensor_tensor(
                        mod[:, s].rearrange("p (g j) r -> p g j r", j=2)[:, :, j, :], rows,
                        bias.broadcast_to([P, 4, ROWS]), ALU.add)
                if s not in SCALE and s not in (GATE[0], GATE[2]):
                    ins.then_inc(mod_ready, 1)
                    dve.wait_ge(mod_ready, s + 1)
                    return
                ins.then_inc(mod_step, 1)
                mod_steps[0] += 1
                dve.wait_ge(mod_step, mod_steps[0])
                if s in SCALE:
                    n = SCALE.index(s)
                    g = col(V_G + KD * n, KD).unsqueeze(2).broadcast_to([P, KD, ROWS])
                    nc.vector.scalar_tensor_tensor(gain[:, n], mod[:, s], 1.0, g, ALU.add, ALU.mult).then_inc(mod_ready, 1)
                else:
                    nc.vector.tensor_scalar(mod[:, s], mod[:, s], 0.5, None, ALU.mult).then_inc(mod_ready, 1)
                dve.wait_ge(mod_ready, s + 1)

            def add_square(n, c):
                if 0 < c < KD - 1:
                    dve.wait_ge(sq_ready, KD * n + c + 1)
                if c == 1:
                    nc.vector.tensor_tensor(acc[:], sq[:, 0, :], sq[:, 1, :], ALU.add).then_inc(sq_used, 2)
                elif 1 < c < KD - 1:
                    dve.wait_ge(sq_used, (KD - 1) * n + c)
                    nc.vector.tensor_tensor(acc[:], acc[:], sq[:, c % 2, :], ALU.add).then_inc(sq_used, 1)

            def inverse(n):
                dve.wait_ge(std_ready, n + 1)
                nc.vector.reciprocal(rms[:, 1, :], rms[:, 0, :]).then_inc(rstd_ready, 1)

            def apply_norm(n):
                dve.wait_ge(r_ready, n + 1)
                r = by_half(r_ps)

                def scale_samples(c):
                    if c >= 2:
                        dve.wait_ge(norm_fs, KD * n + c - 1)
                    nc.vector.tensor_tensor(sample(by_half(sq[:, c % 2, :])), sample(by_half(x[:, c, :])), sample(r),
                                            ALU.mult).then_inc(norm_s1, 1)

                def low(c):
                    dve.wait_ge(hm_hi_ready, KD * n + c + 1)
                    nc.vector.tensor_tensor(hm_lo[:, c, :], full[:, c % 2, :], hm_hi[:, c, :].bitcast(F32),
                                            ALU.subtract).then_inc(hm_lo_ready[0], 1)

                scale_samples(0)
                for c in range(KD):
                    q = KD * n + c
                    t, f = by_half(sq[:, c % 2, :]), by_half(full[:, c % 2, :])
                    if c >= 2:
                        dve.wait_ge(norm_f, q - 1)
                    nc.vector.scalar_tensor_tensor(prompt(t), prompt(by_half(x[:, c, :])), gain[:, n, c, 0:1],
                                                   prompt(r), ALU.mult, ALU.mult).then_inc(norm_t, 1)
                    dve.wait_ge(norm_s1, q + 1)
                    nc.vector.tensor_tensor(steps(sample(t)), steps(sample(t)), over_steps(gain[:, n, c, 1:ROWS]),
                                            ALU.mult).then_inc(norm_s2, 1)
                    if c + 1 < KD:
                        scale_samples(c + 1)
                    if c >= 2:
                        dve.wait_ge(*lo_at(n, c - 2))
                    dve.wait_ge(norm_s2, q + 1)
                    nc.vector.tensor_tensor(steps(sample(f)), steps(sample(t)),
                                            over_steps(mod[:, SHIFT[n], c, 1:ROWS]), ALU.add).then_inc(norm_fs, 1)
                    if c % 2:
                        low(c - 1)

            def up_unit(u, side, local, before):
                dve.wait_ge(tile_done[1], u + 1)
                dve.wait_ge(tile_read[0], u + 1)
                nc.vector.tensor_tensor(by_half(full[:, side, :]), by_half(sil[:]), halves(tile_b),
                                        ALU.mult).then_inc(tile_read[1], 1)
                dve.wait_ge(h_hi_ready, before + local + 1)
                nc.vector.tensor_tensor(h_lo[:, local, :], full[:, side, :], h_hi[:, local, :].bitcast(F32),
                                        ALU.subtract).then_inc(h_lo_ready, 1)

            def residual(u, m, t, e, s):
                ps = tiles[t]
                xm = by_half(x[:, m, :]) if isinstance(m, int) else by_half(x[:, bass.ds(m, 1), :].rearrange("p o n -> p (o n)"))
                dve.wait_ge(tile_done[t], u + 1)
                g = steps(gated[:, t, :].rearrange("p (h n) -> p h n", h=2))
                nc.vector.tensor_tensor(g, steps(sample(ps)), over_steps(gate_rows(s, m)), ALU.mult).then_inc(gate_tmp, 1)
                nc.vector.scalar_tensor_tensor(prompt(xm), prompt(ps), gate_prompt(s, m), prompt(xm), ALU.mult,
                                               ALU.add).then_inc(tile_read[t], 1)
                dve.wait_ge(gate_tmp, e + 1)
                nc.vector.tensor_tensor(steps(sample(xm)), steps(sample(xm)), g, ALU.add).then_inc(x_ready, 1)

            def gate_rows(s, m):
                return mod[:, s, m, 1:ROWS] if isinstance(m, int) else mod[:, s, bass.ds(m, 1), 1:ROWS].rearrange("p o r -> p (o r)")

            def gate_prompt(s, m):
                return mod[:, s, m, 0:1] if isinstance(m, int) else mod[:, s, bass.ds(m, 1), 0:1].rearrange("p o r -> p (o r)")

            def down_unit(u, i, e0, s):
                for t in range(2):
                    residual(u, i * 2 + t, t, e0 + i * 2 + t, s)

            def down_and_squares(first_unit, e0, s, n):
                for i in range(KD // 2):
                    u = first_unit + i
                    residual(u, 2 * i, 0, e0 + 2 * i, s)
                    if i:
                        add_square(n, 2 * i - 1)
                    residual(u, 2 * i + 1, 1, e0 + 2 * i + 1, s)
                    if i:
                        add_square(n, 2 * i)
                add_square(n, KD - 1)

            def ffn(f, gate, norm_after, between):
                for part, n, up, down, before, e0 in FFNS[f]:
                    pairs_and(dve, n, lambda i, side: up_unit(up + i, side, i, before), between[part])
                    if part < len(FF_PARTS) - 1:
                        pairs(dve, KD // 2, lambda i, side: down_unit(down + i, i, e0, gate))
                    else:
                        down_and_squares(down, e0, gate, norm_after)
                inverse(norm_after)

            for c in range(KD):
                add_square(0, c)
            inverse(0)
            mod_evacuate(0)
            mod_evacuate(1)
            apply_norm(0)
            ffn(0, GATE[0], 1, ({4: lambda: mod_evacuate(2)}, {4: lambda: mod_evacuate(3)}, {3: lambda: mod_evacuate(4)}))
            apply_norm(1)

            def glu(c):
                u = GLU + c
                if c == 0:
                    dve.wait_ge(pads_ready, 1)
                    dve.wait_ge(state_in, 32)
                dve.wait_ge(tile_read[0], u + 1)
                dve.wait_ge(tile_done[1], u + 1)
                s = by_half(sil[:])
                nc.vector.tensor_tensor(split2(conv_p[:, c, CONV_PAD:]), prompt(s), prompt(tile_b),
                                        ALU.mult)
                nc.vector.tensor_tensor(split2(conv_s[:, c, CONV_PAD * DEC_BATCH:]), sample(s), sample(tile_b),
                                        ALU.mult).then_inc(tile_read[1], 1)

            def window(c, k):
                if isinstance(k, int):
                    return (split2(conv_p[:, c, k:k + SEQ]),
                            split2(conv_s[:, c, DEC_BATCH * k:DEC_BATCH * (k + DEC_SEQ)]), col(V_WDW + c * WIDTH + k))
                return (split2(conv_p[:, c, bass.ds(k, SEQ)]),
                        split2(conv_s[:, c, bass.ds(k * DEC_BATCH, DEC_BATCH * DEC_SEQ)]),
                        vec[:, bass.ds(k + (V_WDW + c * WIDTH), 1)])

            def conv_start(c):
                vc = by_half(v[:, c, :])
                win_p, win_s, w = window(c, 0)
                dve.wait_ge(tile_read[1], GLU + c + 1)
                nc.vector.tensor_scalar(prompt(vc), win_p, w, col(V_BDW + c), ALU.mult, ALU.add).then_inc(conv_tap, 1)
                nc.vector.tensor_scalar(sample(vc), win_s, w, col(V_BDW + c), ALU.mult, ALU.add).then_inc(conv_tap, 1)

            def conv_taps(c, g0, g1):
                vc = by_half(v[:, c, :])
                with dve.Fori(g0, g1) as g:
                    for kk in range(TAPS_PER_LOOP):
                        k = g * TAPS_PER_LOOP + (kk + 1)
                        done = g * (2 * TAPS_PER_LOOP) + 2 * (kk + 1 + c * WIDTH)
                        win_p, win_s, w = window(c, k)
                        dve.wait_ge(conv_tap, done - 1)
                        nc.vector.scalar_tensor_tensor(prompt(vc), win_p, w, prompt(vc), ALU.mult,
                                                       ALU.add).then_inc(conv_tap, 1)
                        dve.wait_ge(conv_tap, done)
                        nc.vector.scalar_tensor_tensor(sample(vc), win_s, w, sample(vc), ALU.mult,
                                                       ALU.add).then_inc(conv_tap, 1)

            glu(0)
            mod_evacuate(5)
            conv_start(0)
            conv_taps(0, 0, TAP_GROUPS // 2)
            glu(1)
            conv_taps(0, TAP_GROUPS // 2, TAP_GROUPS)
            glu(2)
            conv_start(1)
            conv_taps(1, 0, TAP_GROUPS // 2)
            glu(3)
            conv_taps(1, TAP_GROUPS // 2, TAP_GROUPS)
            conv_start(2)
            conv_taps(2, 0, TAP_GROUPS)
            mod_evacuate(6)
            mod_evacuate(7)
            conv_start(3)
            conv_taps(3, 0, TAP_GROUPS)
            dve.wait_ge(ln_sum_done, 1)
            for c in range(CONV_CHUNKS):
                vc = by_half(v[:, c, :])
                nc.vector.scalar_tensor_tensor(vc, halves(stat_ps), -1.0 / D_CONV, vc, ALU.mult,
                                               ALU.add).then_inc(ln_centred, 1)
            dve.wait_ge(ln_std_ready, 1)
            dve.wait_ge(pmix_lo_ready, GROUPS)
            nc.vector.reciprocal(rstd[:], acc[:]).then_inc(ln_rstd_ready, 1)
            dve.wait_ge(ln_rstd_ready, 1)
            for c in range(CONV_CHUNKS):
                nc.vector.tensor_tensor(v[:, c, :], v[:, c, :], rstd[:], ALU.mult).then_inc(ln_scaled, 1)
            for c in range(CONV_CHUNKS):
                dve.wait_ge(vmix_hi_ready, c + 1)
                nc.vector.tensor_tensor(hm_lo[:, GROUPS + c, :], (full, sq)[c // 2][:, c % 2, :],
                                        hm_hi[:, GROUPS + c, :].bitcast(F32), ALU.subtract).then_inc(vmix_lo_ready, 1)
            dve.wait_ge(mod_ready, 8)
            down_and_squares(OUT, OUT_TILES, GATE[1], 2)
            inverse(2)
            apply_norm(2)
            ffn(1, GATE[2], 3, ({1: lambda: mod_evacuate(8)}, {}, {}))
            dve.wait_ge(r_ready, 4)
            for c in range(KD):
                nc.vector.scalar_tensor_tensor(x[:, c, :], x[:, c, :], col(V_GF + c), r_ps, ALU.mult,
                                               ALU.mult).then_inc(y_ready, 1)

        @block.gpsimd
        def _(pool):
            def split_lo(u, side):
                pool.wait_ge(w_hi_ready, u + 1)
                nc.gpsimd.tensor_tensor(w_lo[:, side, :], w_raw[:, side, :], w_hi[:, side, :].bitcast(F32),
                                        ALU.subtract).then_inc(w_lo_ready, 1)

            def hm_lows(n, next_unit):
                side = next_unit % 2

                def half(m):
                    cols = slice(m * UNIT // 2, (m + 1) * UNIT // 2)
                    return nc.gpsimd.tensor_tensor(w_lo[:, side, cols], w_raw[:, side, cols],
                                                   w_hi[:, side, cols].bitcast(F32), ALU.subtract)

                if n:
                    pool.wait_ge(w_hi_ready, next_unit + 1)
                    half(0)
                for c in range(1, KD, 2):
                    pool.wait_ge(hm_hi_ready, KD * n + c + 1)
                    nc.gpsimd.tensor_tensor(hm_lo[:, c, :], full[:, c % 2, :], hm_hi[:, c, :].bitcast(F32),
                                            ALU.subtract).then_inc(hm_lo_ready[1], 1)
                if n == 0:
                    pool.wait_ge(w_hi_ready, next_unit + 1)
                    half(0)
                half(1).then_inc(w_lo_ready, 1)

            def split_pairs(first, last):
                with pool.Fori(first // 2, last // 2) as i:
                    for side in range(2):
                        split_lo(i * 2 + side, side)

            nc.gpsimd.memset(cond[:], 0.0).then_inc(zeroed, 1)
            nc.gpsimd.memset(ident[:], 0.0).then_inc(ident_zero, 1)
            nc.gpsimd.memset(ones[:], 1.0)
            for t in range(POOL_PAD):
                nc.gpsimd.memset(small[:, t:t + 1], 1.0 / (t + 1))
            nc.gpsimd.memset(scrap, 0.0)
            nc.gpsimd.memset(eps, EPS).then_inc(consts_ready, 1)
            pool.wait_ge(ident_zero, 1)
            nc.gpsimd.affine_select(out=ident[:], in_=ident[:], compare_op=ALU.not_equal, fill=1.0, base=0,
                                    pattern=[[-1, P]], channel_multiplier=1).then_inc(ident_ready, 1)
            split_lo(0, 0)
            hm_lows(0, 1)
            split_pairs(2, GLU)
            split_lo(GLU, 0)
            hm_lows(1, GLU + 1)
            pool.wait_ge(tile_done[1], GLU)
            nc.gpsimd.memset(conv_p[:, :, 0:CONV_PAD], 0.0)
            nc.gpsimd.memset(pool_p[:, :, 0:POOL_PAD], 0.0).then_inc(pads_ready, 1)
            for u in range(GLU + 2, GLU + 6):
                split_lo(u, u % 2)
            pool.wait_ge(wp_hi_ready, 1)
            nc.gpsimd.tensor_tensor(wp_lo[:], wp_raw[:], wp_hi[:].bitcast(F32), ALU.subtract).then_inc(wp_lo_ready, 1)

            def window_sums(g):
                pool.wait_ge(tile_read[g % 2], POOL_IN + g // 2 + 1)
                src_p, src_s = pool_p[:, g, :], pool_s[:, g, :]
                for level in range(g + 1):
                    d = 1 << level
                    first = 2 * d - 1
                    dst = sums[:, level % 2, :]
                    dst_p, dst_s = dst[:, 0:POOL_P], dst[:, POOL_P:]
                    if level:
                        pool.wait_ge(pool_step, steps_done[0])
                    nc.gpsimd.tensor_tensor(dst_p[:, first:POOL_P], src_p[:, first:POOL_P],
                                            src_p[:, first - d:POOL_P - d], ALU.add)
                    a, b, n = first * DEC_BATCH, (first - d) * DEC_BATCH, POOL_S - first * DEC_BATCH
                    ins = nc.gpsimd.tensor_tensor(dst_s[:, a:a + n], src_s[:, a:a + n], src_s[:, b:b + n], ALU.add)
                    if level < g:
                        ins.then_inc(pool_step, 1)
                        steps_done[0] += 1
                    else:
                        ins.then_inc(window_ready, 1)
                    src_p, src_s = dst_p, dst_s

            def window_means(g):
                pool.wait_ge(window_ready, g + 1)
                pool.wait_ge(scaled_ready, g + 1)
                m = mean_in[g % 2]
                n = WINDOWS[g] - 1
                nc.gpsimd.tensor_tensor(m[:, 0:n], sums[:, g % 2, POOL_PAD:POOL_PAD + n], small[:, 0:n],
                                        ALU.mult).then_inc(pool_step, 1)
                steps_done[0] += 1
                pool.wait_ge(pool_step, steps_done[0])
                mh = by_half(m[:])
                nc.gpsimd.tensor_tensor(prompt(mh), prompt(mh), split2(pool_p[:, g, POOL_PAD:]), ALU.subtract)
                nc.gpsimd.tensor_tensor(sample(mh), sample(mh), split2(pool_s[:, g, POOL_PAD * DEC_BATCH:]),
                                        ALU.subtract).then_inc(pooled_ready, 1)
                pool.wait_ge(pooled_hi_ready, g + 1)
                nc.gpsimd.tensor_tensor(pooled_lo[:, g % 2, :], m[:], pooled_hi[:, g % 2, :].bitcast(F32),
                                        ALU.subtract).then_inc(pooled_lo_ready, 1)

            steps_done = [0]
            for g in range(GROUPS):
                if g % 2 == 0:
                    split_lo(OUT + g // 2, g // 2)
                window_sums(g)
                window_means(g)
            for g in range(GROUPS):
                pool.wait_ge(pmix_hi_ready, g + 1)
                nc.gpsimd.tensor_tensor(hm_lo[:, g, :], full[:, g % 2, :], hm_hi[:, g, :].bitcast(F32),
                                        ALU.subtract).then_inc(pmix_lo_ready, 1)
            for u in range(OUT + 2, FFN2 + 1):
                split_lo(u, u % 2)
            hm_lows(2, FFN2 + 1)
            split_pairs(FFN2 + 2, UNITS)


def column_units(w, tiles):
    import numpy as np

    k = w.shape[0] // P
    blocks = w.reshape(k, P, w.shape[1] // P, P)
    out = np.zeros((len(tiles), P, UNIT), w.dtype)
    for n, (a, b) in enumerate(tiles):
        both = np.stack([blocks[:, :, a], blocks[:, :, b]], axis=1)
        out[n, :, :2 * k * P] = both.transpose(2, 0, 1, 3).reshape(P, 2 * k * P)
    return out


def ffn_units(up, down):
    import numpy as np

    n_hidden, first, units = D_FF // P, 0, []
    pairs_out = [(m, m + 1) for m in range(0, KD, 2)]
    for n in FF_PARTS:
        units.append(column_units(up, [(f, n_hidden + f) for f in range(first, first + n)]))
        units.append(column_units(down[first * P:(first + n) * P], pairs_out))
        first += n
    return np.concatenate(units)


def to_halves(xp, xs):
    import numpy as np

    steps = xs.transpose(1, 0, 2).reshape(2, HALF_STEPS * DEC_BATCH, -1)
    both = np.concatenate([xp.reshape(2, HALF_PROMPT, -1), steps], axis=1)
    return both.reshape(TOKENS, -1).T


def chunks(a):
    return a.reshape(a.shape[0] // P, P, *a.shape[1:]).swapaxes(0, 1)


def kernel(**inputs):
    import numpy as np
    import concourse.bacc as bacc
    from concourse.bass_utils import run_bass_kernel_spmd

    a = {k: np.asarray(t) for k, t in inputs.items()}
    pairs_out = [(m, m + 1) for m in range(0, KD, 2)]
    w_in = a["w_in"][0]
    mixed_rows = np.concatenate([a["w_out"][0][D_CONV:], a["w_out"][0][:D_CONV]])
    units = np.concatenate([
        ffn_units(a["w_ffn1_up"][0], a["w_ffn1_down"][0]),
        column_units(w_in, [(CONV_CHUNKS + c, c) for c in range(CONV_CHUNKS)]),
        column_units(w_in, [(2 * CONV_CHUNKS + g, 2 * CONV_CHUNKS + g + 1) for g in range(0, GROUPS, 2)]),
        column_units(mixed_rows, pairs_out),
        ffn_units(a["w_ffn2_up"][0], a["w_ffn2_down"][0])])
    w_ada = a["w_ada"][0].reshape(ADA_QUARTERS, 2, P, N_MOD, D_MODEL).transpose(3, 0, 2, 1, 4)
    w_ada = w_ada.reshape(N_MOD * ADA_QUARTERS, P, 2, D_MODEL)
    cond = np.concatenate([a["c_prompt"], a["c_sample"]])
    vectors = np.concatenate(
        [chunks(a["b_ada"][0])] + [chunks(a[n][0]) for n in ("g_ffn1", "g_mix", "g_ffn2")] + [chunks(a["g_final"])]
        + [chunks(a[n][0]) for n in ("ln_g", "ln_b", "b_dw", "pool_scale")]
        + [chunks(a["w_dw"][0].T).reshape(P, -1), chunks(cond.T).reshape(P, -1)], axis=1)
    arrays = {
        "x_in": chunks(to_halves(a["x_prompt"][0], a["x_sample"])),
        "w_units": units,
        "w_ada": w_ada,
        "w_pool": a["w_pool"][0].transpose(1, 0, 2).reshape(P, GROUPS * P),
        "vectors": vectors,
        "conv_state": chunks(a["state_conv"][0].transpose(2, 1, 0).reshape(D_CONV, -1)),
        "pool_state": chunks(a["state_pool"][0].transpose(2, 1, 0).reshape(D_POOL, -1)),
    }
    arrays = {k: np.ascontiguousarray(t) for k, t in arrays.items()}
    outs = {"y_out": (P, KD, TOKENS), "conv_p_out": (P, CONV_CHUNKS, CONV_PAD), "pool_p_out": (P, GROUPS, POOL_PAD),
            "conv_s_out": (P, CONV_CHUNKS, CONV_PAD * DEC_BATCH), "pool_s_out": (P, GROUPS, POOL_PAD * DEC_BATCH)}
    nc = bacc.Bacc("TRN2", target_bir_lowering=False, num_devices=1)
    args = [nc.dram_tensor(k, t.shape, mybir.dt.from_np(t.dtype), kind="ExternalInput").ap() for k, t in arrays.items()]
    args += [nc.dram_tensor(k, s, F32, kind="ExternalOutput").ap() for k, s in outs.items()]
    trunk(nc, *args)
    got = run_bass_kernel_spmd(nc, [arrays], core_ids=[0]).results[0]

    def rows(name):
        t = np.asarray(got[name])
        return t.transpose(2, 1, 0).reshape(t.shape[2], -1)

    y = rows("y_out").reshape(2, HALF, D_MODEL)
    y_sample = y[:, HALF_PROMPT:].reshape(DEC_SEQ, DEC_BATCH, D_MODEL).swapaxes(0, 1)
    return (np.ascontiguousarray(y[:, :HALF_PROMPT].reshape(1, SEQ, D_MODEL)),
            np.ascontiguousarray(y_sample),
            np.ascontiguousarray(rows("conv_p_out")[None, None]),
            np.ascontiguousarray(rows("pool_p_out")[None, None]),
            np.ascontiguousarray(rows("conv_s_out").reshape(CONV_PAD, DEC_BATCH, D_CONV).swapaxes(0, 1)[None]),
            np.ascontiguousarray(rows("pool_s_out").reshape(POOL_PAD, DEC_BATCH, D_POOL).swapaxes(0, 1)[None]))
```

```python
from contextlib import ExitStack

import concourse.bass as bass
from concourse import mybir

F32 = mybir.dt.float32
F32R = mybir.dt.float32r
ALU = mybir.AluOpType
ACT = mybir.ActivationFunctionType

P = 128
D_MODEL = 1024
SEQ = 512
DEC_BATCH = 8
DEC_SEQ = 8
D_CONV = 512
D_POOL = 512
WIDTH = 31
WINDOWS = (2, 4, 8, 16)
POOL_MAX = max(WINDOWS)
D_FF = 2816
N_MOD = 9
EPS = 1e-6

KD = D_MODEL // P
CONV_CHUNKS = D_CONV // P
GROUPS = len(WINDOWS)
ROWS = 1 + DEC_BATCH
TOKENS = SEQ + DEC_SEQ * DEC_BATCH
HALF = TOKENS // 2
HALF_PROMPT = SEQ // 2
HALF_STEPS = DEC_SEQ // 2

TOKEN_BLOCKS = -(-TOKENS // P)

UNIT = 16 * P
FF_PARTS = (8, 8, 6)
FFN_UNITS = sum(FF_PARTS) + len(FF_PARTS) * KD // 2
FFN1 = 0
MIX = FFN1 + FFN_UNITS
GLU = tuple(MIX + n for n in (0, 2, 4, 5))
POOL_IN = tuple(MIX + n for n in (1, 3))
OUT = MIX + len(GLU) + len(POOL_IN)
FFN2 = OUT + KD // 2
UNITS = FFN2 + FFN_UNITS

CONV_PAD = WIDTH - 1
POOL_PAD = POOL_MAX - 1
CONV_P = CONV_PAD + SEQ
CONV_S = (CONV_PAD + DEC_SEQ) * DEC_BATCH
POOL_P = POOL_PAD + SEQ
POOL_S = (POOL_PAD + DEC_SEQ) * DEC_BATCH
TAPS_PER_LOOP = 5
TAP_GROUPS = (WIDTH - 1) // TAPS_PER_LOOP
PE_BATCHES = 5
PE_TAP0 = WIDTH - PE_BATCHES * TAPS_PER_LOOP
DVE_TAPS = (CONV_CHUNKS - 1) * WIDTH + PE_TAP0

Y_POOL = (KD - 2, KD - 1)

ADA_SLOTS = 3
ADA_QUARTERS = 4
ADA_N = D_MODEL // 4
SHIFT = (0, 3, 6)
SCALE = (1, 4, 7)
GATE = (2, 5, 8)

V_ADA, V_G, V_GF = 0, 72, 96
V_LNG, V_LNB, V_BDW, V_PSC = 104, 108, 112, 116
V_WDW = 120
V_COND = V_WDW + CONV_CHUNKS * WIDTH
V_ALL = V_COND + KD * ROWS


def trunk(nc, x_in, w_units, w_ada, w_pool, vectors, conv_state, pool_state,
          y_out, conv_p_out, pool_p_out, conv_s_out, pool_s_out):
    ctx = ExitStack()
    with ctx:
        def sb(name, shape, dt=F32):
            return ctx.enter_context(nc.sbuf_tensor(name, shape, dt))

        def sem(name):
            return ctx.enter_context(nc.semaphore(name))

        with nc.sbuf_tensor("h_hi", [P, 8, TOKENS], F32R) as h_hi, \
                nc.sbuf_tensor("h_lo", [P, 8, TOKENS], F32R) as h_lo:
            pass
        with ExitStack() as under:
            def alias(name, shape, dt=F32):
                return under.enter_context(nc.sbuf_tensor(name, shape, dt))
            conv_p = alias("conv_p", [P, CONV_CHUNKS, CONV_P])
            v = alias("v", [P, CONV_CHUNKS, TOKENS])
            pool_p = alias("pool_p", [P, GROUPS, POOL_P])
            sums = alias("sums", [P, 2, POOL_P + POOL_S])
            wp_hi = alias("wp_hi", [P, GROUPS * P], F32R)
            wp_lo = alias("wp_lo", [P, GROUPS * P], F32R)
        ctx.enter_context(nc.sbuf_tensor("h_room", [P, 2 * 8 * TOKENS], F32))

        x = sb("x", [P, KD, TOKENS])
        hm_hi = sb("hm_hi", [P, KD, TOKENS], F32R)
        hm_lo = sb("hm_lo", [P, KD, TOKENS], F32R)
        w_raw = sb("w_raw", [P, 2, UNIT])
        w_hi = sb("w_hi", [P, 2, UNIT], F32R)
        w_lo = sb("w_lo", [P, 2, UNIT], F32R)
        ada_raw = sb("ada_raw", [P, ADA_SLOTS, 2, D_MODEL])
        vec = sb("vec", [P, V_ALL])
        cond = sb("cond", [P, KD, 32])
        ident = sb("ident", [P, P])
        sel = sb("sel", [P, 3, 32])
        ones = sb("ones", [P, P])
        small = sb("small", [P, POOL_PAD + 2])
        rms = sb("rms", [P, 2, TOKEN_BLOCKS])
        ada_rows = sb("ada_rows", [P, ADA_N])
        mod = sb("mod", [P, N_MOD, KD, ROWS])
        gain = sb("gain", [P, 3, KD, ROWS])
        sil = sb("sil", [P, TOKENS])
        full = sb("full", [P, 2, TOKENS])
        sq = sb("sq", [P, 2, TOKENS])
        acc = sb("acc", [P, TOKENS])
        mean_b = sb("mean_b", [P, TOKENS])
        diag = sb("diag", [P, TAPS_PER_LOOP, P])
        gated = sb("gated", [P, 2, HALF_STEPS * DEC_BATCH * 2])
        conv_s = sb("conv_s", [P, CONV_CHUNKS, CONV_S])
        pool_s = sb("pool_s", [P, GROUPS, POOL_S])
        wp_raw = sb("wp_raw", [P, GROUPS * P])
        pooled_hi = sb("pooled_hi", [P, 2, TOKENS], F32R)
        pooled_lo = sb("pooled_lo", [P, 2, TOKENS], F32R)
        mean_in = [acc, mean_b]
        four = [full[:, 0, :], full[:, 1, :], sq[:, 0, :], sq[:, 1, :]]
        eps, scrap = small[:, POOL_PAD:POOL_PAD + 1], small[:, POOL_PAD + 1:POOL_PAD + 2]

        def bank2(name):
            return ctx.enter_context(nc.psum_tensor(name, [P, 2, 512], F32))
        tile_a, tile_b, stat_ps, ada_ps = (bank2(n) for n in ("tile_a", "tile_b", "stat_ps", "ada_ps"))
        tiles = (tile_a, tile_b)

        def first_ps(c, j):
            return ada_ps[:, c % 2, ADA_N + ROWS * j:ADA_N + ROWS * (j + 1)]

        r_ps = stat_ps.rearrange("p h n -> p (h n)")[:, 0:TOKENS]
        ln_sums_ps = ada_ps[:, 0, 512 - TOKEN_BLOCKS:512]
        sums_ps = stat_ps[:, 1, 512 - TOKEN_BLOCKS:512]

        vec_in, state_in, wp_in = sem("vec_in"), sem("state_in"), sem("wp_in")
        x_in_sem = [sem(f"x_in_sem{n}") for n in range(KD // 2)]
        w_raw_ready = [sem("w_raw_ready0"), sem("w_raw_ready1")]
        ada_raw_ready = [sem(f"ada_raw_ready{n}") for n in range(ADA_SLOTS)]
        state_out, y_sent = sem("state_out"), sem("y_sent")
        zeroed, ident_zero, ident_ready, consts_ready, cond_ready = (
            sem("zeroed"), sem("ident_zero"), sem("ident_ready"), sem("consts_ready"), sem("cond_ready"))
        ada_used, ada_copied, ada_turned = sem("ada_used"), sem("ada_copied"), sem("ada_turned")
        mod_step, mod_ready = sem("mod_step"), sem("mod_ready")
        w1_half_ready = sem("w1_half_ready")
        first_added, first_ready = sem("first_added"), sem("first_ready")
        sel_step, sel_ready = sem("sel_step"), sem("sel_ready")
        w_hi_ready, w_lo_ready = sem("w_hi_ready"), sem("w_lo_ready")
        tile_done = (sem("tile_a_done"), sem("tile_b_done"))
        tile_read = (sem("tile_a_read"), sem("tile_b_read"))
        h_hi_ready, h_lo_ready = sem("h_hi_ready"), sem("h_lo_ready")
        gate_tmp, x_ready = sem("gate_tmp"), sem("x_ready")
        sq_ready, sq_used, stat_done, std_ready, rstd_ready = (
            sem("sq_ready"), sem("sq_used"), sem("stat_done"), sem("std_ready"), sem("rstd_ready"))
        r_ready, norm_s1, norm_s2 = sem("r_ready"), sem("norm_s1"), sem("norm_s2")
        norm_t, norm_fs, norm_f = sem("norm_t"), sem("norm_fs"), sem("norm_f")
        hm_hi_ready, y_ready = sem("hm_hi_ready"), sem("y_ready")
        r_copy_ready = sem("r_copy_ready")
        y_scaled, y_pool_ready = sem("y_scaled"), sem("y_pool_ready")
        hm_lo_ready = (sem("hm_lo_even_ready"), sem("hm_lo_odd_ready"))
        pads_ready, conv_tap = sem("pads_ready"), sem("conv_tap")
        pool_step, window_ready, scaled_ready, pooled_ready = (
            sem("pool_step"), sem("window_ready"), sem("scaled_ready"), sem("pooled_ready"))
        wp_hi_ready, wp_lo_ready = sem("wp_hi_ready"), sem("wp_lo_ready")
        pooled_hi_ready, pooled_lo_ready = sem("pooled_hi_ready"), sem("pooled_lo_ready")
        pmix_done, pmix_full, pmix_hi_ready, pmix_lo_ready = (
            sem("pmix_done"), sem("pmix_full"), sem("pmix_hi_ready"), sem("pmix_lo_ready"))
        diag_ready, diag_used, pe_taps_added = sem("diag_ready"), sem("diag_used"), sem("pe_taps_added")
        ln_sum_done, ln_centred, ln_sq_ready, ln_var_mm = (
            sem("ln_sum_done"), sem("ln_centred"), sem("ln_sq_ready"), sem("ln_var_mm"))
        ln_sq_added = sem("ln_sq_added")
        ln_std_ready, ln_rstd_ready, ln_r_ready, ln_scaled = (
            sem("ln_std_ready"), sem("ln_rstd_ready"), sem("ln_r_ready"), sem("ln_scaled"))
        vmix_full, vmix_hi_ready, vmix_lo_ready = sem("vmix_full"), sem("vmix_hi_ready"), sem("vmix_lo_ready")

        def halves(ps):
            return ps[:, :, 0:HALF]

        def by_half(t):
            return t.rearrange("p (h n) -> p h n", h=2)

        def prompt(t):
            return t[:, :, 0:HALF_PROMPT]

        def sample(t):
            return t[:, :, HALF_PROMPT:HALF]

        def steps(t):
            return t.rearrange("p h (t b) -> p h t b", b=DEC_BATCH)

        def over_steps(rows):
            return rows.unsqueeze(1).unsqueeze(1).broadcast_to([P, 2, HALF_STEPS, DEC_BATCH])

        def split2(t):
            return t.rearrange("p (h n) -> p h n", h=2)

        def col(a, n=1):
            return vec[:, a:a + n]

        def ffn_parts(first_unit, ffn):
            u, out = first_unit, []
            for part, n in enumerate(FF_PARTS):
                before = ffn * sum(FF_PARTS) + sum(FF_PARTS[:part])
                tiles_before = ffn * (len(FF_PARTS) + 1) * KD + part * KD
                out.append((part, n, u, u + n, before, tiles_before))
                u += n + KD // 2
            return out

        FFNS = (ffn_parts(FFN1, 0), ffn_parts(FFN2, 1))
        OUT_TILES = len(FF_PARTS) * KD
        NORM_TILES = (0, OUT_TILES, OUT_TILES + KD, 2 * OUT_TILES + KD)

        def pairs(eng, count, body, first=0):
            if count // 2 - first == 1:
                for side in range(2):
                    body(2 * first + side, side)
            elif count // 2 > first:
                with eng.Fori(first, count // 2) as i:
                    for side in range(2):
                        body(i * 2 + side, side)

        def pairs_and(eng, count, body, between, first=0):
            for stop in sorted(set(between) | {count // 2}):
                pairs(eng, 2 * stop, body, first)
                first = max(first, stop)
                if stop in between:
                    between[stop]()

        def lo_at(n, c):
            return hm_lo_ready[c % 2], KD // 2 * n + c // 2 + 1

        def mod_at(s):
            return mod_ready, s - 1

        def copies(s):
            return KD + s - 1

        block = ctx.enter_context(nc.Block())

        @block.sync
        def _(sp):
            sp.dma_start(vec[:], vectors).then_inc(vec_in, 16)
            for c in range(0, KD, 2):
                sp.dma_start(x[:, c:c + 2, :], x_in[:, c:c + 2, :]).then_inc(x_in_sem[c // 2], 16)
            sp.dma_start(w_raw[:, 0, :], w_units[0]).then_inc(w_raw_ready[0], 16)
            for a in range(KD):
                if a >= ADA_SLOTS:
                    sp.wait_ge(ada_used, a - ADA_SLOTS + 1)
                sp.dma_start(ada_raw[:, a % ADA_SLOTS], w_ada[a]).then_inc(ada_raw_ready[a % ADA_SLOTS], 16)
            sp.dma_start(w_raw[:, 1, :], w_units[1]).then_inc(w_raw_ready[1], 16)
            sp.dma_start(conv_s[:, :, 0:CONV_PAD * DEC_BATCH], conv_state).then_inc(state_in, 16)
            sp.dma_start(pool_s[:, :, 0:POOL_PAD * DEC_BATCH], pool_state).then_inc(state_in, 16)
            sp.dma_start(wp_raw[:], w_pool).then_inc(wp_in, 16)
            with sp.Fori(1, UNITS // 2) as i:
                for side in range(2):
                    sp.wait_ge(w_lo_ready, i * 2 + (side - 1))
                    sp.dma_start(w_raw[:, side, :], w_units[i * 2 + side]).then_inc(w_raw_ready[side], 16)
            for c in (0, 1, 2, 6, 3, 4, 7, 5):
                if c in Y_POOL:
                    sp.wait_ge(y_pool_ready, Y_POOL.index(c) + 1)
                else:
                    sp.wait_ge(y_ready, c + 1)
                sp.dma_start(y_out[:, c, :], x[:, c, :]).then_inc(y_sent, 16)
            sp.wait_ge(y_sent, 16 * KD)
            sp.wait_ge(state_out, 16 * 4)

        @block.tensor
        def _(pe):
            def ada_products(s, first=0, last=ADA_QUARTERS):
                pe.wait_ge(cond_ready, 1)
                if first == 0:
                    pe.wait_ge(ada_copied, max(KD, copies(s - 2)))
                for q in range(first, last):
                    a = ADA_QUARTERS * s + q
                    pe.wait_ge(ada_raw_ready[a % ADA_SLOTS], 16 * (a // ADA_SLOTS + 1))
                    for kk in range(2):
                        k = 2 * q + kk
                        for g in range(4):
                            mm = pe.matmul(ada_ps[32 * g:32 * g + 32, s % 2, 0:ADA_N], cond[:, k, :],
                                           ada_raw[:, a % ADA_SLOTS, kk, ADA_N * g:ADA_N * (g + 1)],
                                           start=(k == 0), stop=(k == KD - 1))
                    mm.then_inc(ada_used, 1)

            def ada_turn(s):
                pe.wait_ge(ada_copied, copies(s))
                pe.wait_ge(*(mod_at(s - 2) if s >= 4 else (first_ready, KD)))
                for j in range(2):
                    mm = pe.transpose(ada_ps[:, s % 2, ADA_N + P * j:ADA_N + P * (j + 1)],
                                      ada_rows[:, P * j:P * (j + 1)], ident[:])
                mm.then_inc(ada_turned, 1)

            def passes(ps, w_slot, block_col, hi, lo, k, first, last):
                cols = slice(block_col * P, (block_col + 1) * P)
                for n, (w, r) in enumerate(((w_hi, hi), (w_hi, lo), (w_lo, hi))):
                    for h in range(2):
                        mm = pe.matmul(ps[:, h, 0:HALF], w[:, w_slot, cols], r[:, k, HALF * h:HALF * (h + 1)],
                                       start=(first and n == 0), stop=(last and n == 2))
                return mm

            def unit(u, side, kc, hi, lo, hidden=None):
                pe.wait_ge(w_lo_ready, u + 1)
                if hidden is not None:
                    pe.wait_ge(h_lo_ready, hidden - 1)
                for t in range(2):
                    pe.wait_ge(tile_read[t], u)
                    for k in range(kc):
                        if hidden is not None and t == 0 and k == kc - 1:
                            pe.wait_ge(h_lo_ready, hidden)
                        mm = passes(tiles[t], side, 2 * k + t, hi, lo, k, k == 0, k == kc - 1)
                    mm.then_inc(tile_done[t], 1)

            def unit_chunk(u, side, hi, lo, k):
                for t in range(2):
                    mm = passes(tiles[t], side, 2 * k + t, hi, lo, k, k == 0, k == KD - 1)
                    if k == KD - 1:
                        mm.then_inc(tile_done[t], 1)

            def unit_by_chunk(u, side, hi, lo, arrive):
                pe.wait_ge(w_lo_ready, u + 1)
                for t in range(2):
                    pe.wait_ge(tile_read[t], u)
                for k in range(KD):
                    pe.wait_ge(*arrive(k))
                    unit_chunk(u, side, hi, lo, k)

            def column_sums(n):
                pe.wait_ge(consts_ready, 1)
                pe.wait_ge(sq_used, (KD - 1) * (n + 1))
                token_sums(sums_ps, acc, True, False)
                pe.wait_ge(sq_ready, KD * (n + 1))
                token_sums(sums_ps, sq[:, 1, :], False, True).then_inc(stat_done, 1)

            def token_sums(out, part, first, last):
                for j in range(TOKEN_BLOCKS):
                    begin = min(P * j, TOKENS - P)
                    mm = pe.matmul(out[:, j:j + 1], part[:, begin:begin + P], ones[:, 0:1],
                                   start=(first and j == 0), stop=(last and j == TOKEN_BLOCKS - 1))
                return mm

            def spread(out=r_ps):
                for j in range(TOKEN_BLOCKS):
                    first = max(0, P * (j + 1) - TOKENS)
                    mm = pe.transpose(out[:, P * j:P * (j + 1) - first],
                                      rms[first:, 1, j:j + 1].broadcast_to([P - first, P]), ident[first:, first:])
                return mm

            def norm_spread(n):
                pe.wait_ge(ident_ready, 1)
                pe.wait_ge(rstd_ready, n + 1)
                spread().then_inc(r_ready, 1)

            def ffn(f, norm, between):
                for part, n, up, down, before, _ in FFNS[f]:
                    if part == 0:
                        if up:
                            unit_by_chunk(up, 0, hm_hi, hm_lo, lambda k: lo_at(norm, k))
                        unit(up + 1, 1, KD, hm_hi, hm_lo)
                    pairs_and(pe, n, lambda i, side: unit(up + i, side, KD, hm_hi, hm_lo), between[part],
                              first=(part == 0))
                    pairs(pe, KD // 2, lambda i, side: unit(down + i, side, n, h_hi, h_lo, hidden=before + n))

            def pool_product(g):
                pe.wait_ge(wp_lo_ready, 1)
                pe.wait_ge(pooled_lo_ready, g + 1)
                if g:
                    pe.wait_ge(pmix_full, g)
                for n, (w, r) in enumerate(((wp_hi, pooled_hi), (wp_hi, pooled_lo), (wp_lo, pooled_hi))):
                    for h in range(2):
                        mm = pe.matmul(stat_ps[:, h, 0:HALF], w[:, g * P:(g + 1) * P],
                                       r[:, g % 2, HALF * h:HALF * (h + 1)], start=(n == 0), stop=(n == 2))
                mm.then_inc(pmix_done, 1)

            def keep_warm(t, n):
                pe.wait_ge(ident_ready, 1)
                for _ in range(n):
                    pe.transpose(tiles[t][:, 0, 0:P], ident[:], ident[:])

            def first_products(c):
                pe.wait_ge(cond_ready, 1)
                if c >= 2:
                    pe.wait_ge(ada_copied, c - 1)
                    pe.wait_ge(first_added, 2 * (c - 1))
                pe.wait_ge(ada_raw_ready[c % ADA_SLOTS], 16 * (c // ADA_SLOTS + 1))
                raw = ada_raw[:, c % ADA_SLOTS].rearrange("p a (k n) -> p (a k) n", n=2 * P)
                for kk in range(2):
                    for g in range(4):
                        mm = pe.matmul(ada_ps[32 * g:32 * g + 32, c % 2, 0:2 * P], cond[:, 2 * g + kk, :],
                                       raw[:, 2 * g + kk, :], start=(kk == 0), stop=(kk == 1))
                mm.then_inc(ada_used, 1)

            def first_turn(c):
                pe.wait_ge(ada_copied, c + 1)
                pe.wait_ge(sel_ready, 1)
                for j in range(2):
                    mm = pe.matmul(first_ps(c, j), ada_rows[:, P * j:P * (j + 1)], sel[:, 0, 0:ROWS],
                                   start=True, stop=True)
                mm.then_inc(ada_turned, 1)

            def first_unit(c):
                if c == 0:
                    pe.wait_ge(w_lo_ready, 1)
                pe.wait_ge(*lo_at(0, c))
                unit_chunk(0, 0, hm_hi, hm_lo, c)

            keep_warm(0, 68)
            column_sums(0)
            norm_spread(0)
            keep_warm(0, 6)
            for c in range(KD):
                first_products(c)
                if c < 2:
                    keep_warm(0, 8)
                elif c < KD - 1:
                    first_unit(c - 2)
                first_turn(c)
            for c in range(KD - 3, KD):
                first_unit(c)
            ffn(0, 0, ({1: lambda: ada_products(2, 0, 3), 2: lambda: ada_products(2, 3), 4: lambda: ada_turn(2)},
                       {0: lambda: ada_products(3, 0, 3), 2: lambda: ada_products(3, 3), 4: lambda: ada_turn(3)},
                       {0: lambda: ada_products(4, 0, 3), 2: lambda: ada_products(4, 3), 3: lambda: ada_turn(4)}))
            ada_products(5, 0, 2)
            column_sums(1)
            ada_products(5, 2, 3)
            norm_spread(1)
            ada_products(5, 3)
            unit_by_chunk(MIX, 0, hm_hi, hm_lo, lambda k: lo_at(1, k))
            ada_turn(5)
            for u in range(MIX + 1, OUT):
                unit(u, u % 2, KD, hm_hi, hm_lo)
                if u >= OUT - 2:
                    pool_product(u - (OUT - 2))

            def conv_batch(b):
                c = CONV_CHUNKS - 1
                if b == 0:
                    pe.wait_ge(tile_read[1], OUT)
                    pe.wait_ge(tile_read[0], OUT)
                for kk in range(TAPS_PER_LOOP):
                    k = PE_TAP0 + b * TAPS_PER_LOOP + kk
                    pe.wait_ge(diag_ready, b * TAPS_PER_LOOP + kk + 1)
                    pe.matmul(tile_a[:, 0, 0:SEQ], diag[:, kk, :], conv_p[:, c, k:k + SEQ],
                              start=(k == PE_TAP0), stop=(k == WIDTH - 1))
                    mm = pe.matmul(tile_a[:, 1, 0:DEC_BATCH * DEC_SEQ], diag[:, kk, :],
                                   conv_s[:, c, DEC_BATCH * k:DEC_BATCH * (k + DEC_SEQ)],
                                   start=(k == PE_TAP0), stop=(k == WIDTH - 1))
                    mm.then_inc(diag_used, 1)

            def ln_sum(c):
                if c < CONV_CHUNKS - 1:
                    pe.wait_ge(conv_tap, 2 * WIDTH * (c + 1))
                else:
                    pe.wait_ge(pe_taps_added, 2)
                for h in range(2):
                    mm = pe.matmul(stat_ps[:, h, 0:HALF], ones[:], v[:, c, HALF * h:HALF * (h + 1)],
                                   start=(c == 0), stop=(c == CONV_CHUNKS - 1))
                return mm

            ada_products(6, 0, 2)
            conv_batch(0)
            ada_products(6, 2, 3)
            conv_batch(1)
            ada_products(6, 3)
            conv_batch(2)
            pool_product(2)
            conv_batch(3)
            ada_turn(6)
            pool_product(3)
            conv_batch(4)
            pe.wait_ge(pmix_full, GROUPS)
            for c in range(CONV_CHUNKS - 1):
                ln_sum(c)
            ada_products(7, 0, 2)
            ln_sum(CONV_CHUNKS - 1).then_inc(ln_sum_done, 1)
            pe.wait_ge(w_lo_ready, OUT + 1)

            def out_chunk(k):
                pe.wait_ge(*((pmix_lo_ready, k + 1) if k < GROUPS else (vmix_lo_ready, k - GROUPS + 1)))
                unit_chunk(OUT, 0, hm_hi, hm_lo, k)

            ada_products(7, 2, 3)
            out_chunk(0)
            out_chunk(1)
            pe.wait_ge(ln_sq_ready, CONV_CHUNKS)
            token_sums(ln_sums_ps, four[-1], True, False)
            pe.wait_ge(ln_sq_added, CONV_CHUNKS - 2)
            token_sums(ln_sums_ps, acc, False, True).then_inc(ln_var_mm, 1)
            out_chunk(2)
            pe.wait_ge(ln_rstd_ready, 1)
            spread().then_inc(ln_r_ready, 1)
            ada_products(7, 3)
            out_chunk(3)
            ada_turn(7)
            for k in range(GROUPS, KD):
                out_chunk(k)
            unit(OUT + 1, 1, KD, hm_hi, hm_lo)
            pairs(pe, KD // 2, lambda i, side: unit(OUT + i, side, KD, hm_hi, hm_lo), first=1)
            ada_products(8, 0, 2)
            column_sums(2)
            ada_products(8, 2, 3)
            norm_spread(2)
            ada_products(8, 3)
            ffn(1, 2, ({1: lambda: ada_turn(8)}, {}, {}))
            column_sums(3)
            norm_spread(3)
            spread(tile_a.rearrange("p h n -> p (h n)")).then_inc(r_copy_ready, 1)

        @block.scalar
        def _(act):
            def ada_load(a):
                act.wait_ge(ada_used, a - ADA_SLOTS + 1)
                act.dma_start(ada_raw[:, a % ADA_SLOTS], w_ada[a]).then_inc(ada_raw_ready[a % ADA_SLOTS], 16)

            def ada_load_first(s):
                for q in range(ADA_SLOTS):
                    ada_load(ADA_QUARTERS * s + q)

            def ada_copy(s):
                act.wait_ge(ada_used, ADA_QUARTERS * (s + 1))
                act.wait_ge(ada_turned, copies(s) - 1)
                nc.scalar.activation(ada_rows[:], ada_ps[:, s % 2, 0:ADA_N], ACT.Copy).then_inc(ada_copied, 1)

            def split_hi(u, side, first=False):
                act.wait_ge(w_raw_ready[side], 16 * (u // 2 + 1) if isinstance(u, int) else (u - side) * 8 + 16)
                if not first:
                    act.wait_ge(tile_done[1], u - 1)
                nc.scalar.activation(w_hi[:, side, :], w_raw[:, side, :], ACT.Copy).then_inc(w_hi_ready, 1)

            def square(n, c):
                if n == 0:
                    act.wait_ge(x_in_sem[c // 2], 16)
                else:
                    act.wait_ge(x_ready, NORM_TILES[n] - KD + c + 1)
                if c >= 2:
                    act.wait_ge(sq_used, (KD - 1) * n + c - 1)
                nc.scalar.activation(sq[:, c % 2, :], x[:, c, :], ACT.Square).then_inc(sq_ready, 1)

            def load_table(function):
                act.wait_ge(consts_ready, 1)
                nc.scalar.activation(scrap, eps, function)

            def root(n):
                act.wait_ge(stat_done, n + 1)
                nc.scalar.activation(rms[:, 0, :], sums_ps, ACT.Sqrt, scale=1.0 / D_MODEL,
                                     bias=eps).then_inc(std_ready, 1)

            def round_hm(n, c):
                q = KD * n + c
                act.wait_ge(norm_t, q + 1)
                if c >= 2:
                    act.wait_ge(*lo_at(n, c - 2))
                nc.scalar.activation(prompt(by_half(full[:, c % 2, :])), prompt(by_half(sq[:, c % 2, :])),
                                     ACT.Identity, bias=mod[:, SHIFT[n], c, 0:1]).then_inc(norm_f, 1)
                act.wait_ge(norm_f, q + 1)
                act.wait_ge(norm_fs, q + 1)
                nc.scalar.activation(hm_hi[:, c, :], full[:, c % 2, :], ACT.Copy).then_inc(hm_hi_ready, 1)

            def up_unit(u, side, local, before):
                act.wait_ge(tile_done[0], u + 1)
                nc.scalar.activation(by_half(sil[:]), halves(tile_a), ACT.Silu).then_inc(tile_read[0], 1)
                act.wait_ge(tile_read[1], u + 1)
                nc.scalar.activation(h_hi[:, local, :], full[:, side, :], ACT.Copy).then_inc(h_hi_ready, 1)
                split_hi(u + 2, side)

            def norm(n, next_unit):
                root(n)
                split_hi(next_unit, next_unit % 2, first=next_unit < 2)
                for c in range(KD):
                    round_hm(n, c)

            def ffn(f, norm_after, between):
                for part, n, up, down, before, _ in FFNS[f]:
                    pairs_and(act, n, lambda i, side: up_unit(up + i, side, i, before), between[part])
                    if part < len(FF_PARTS) - 1:
                        pairs(act, KD // 2, lambda i, side: split_hi(down + i + 2, side))
                    else:
                        squares(norm_after, down)

            def squares(n, first_unit):
                for i in range(KD // 2):
                    if i == KD // 2 - 1:
                        load_table(ACT.Sqrt)
                    square(n, 2 * i)
                    square(n, 2 * i + 1)
                    if first_unit + i + 2 < UNITS and i < KD // 2 - 1:
                        split_hi(first_unit + i + 2, i % 2)

            def ada_last_quarter(s):
                ada_load(ADA_QUARTERS * s + ADA_QUARTERS - 1)

            act.wait_ge(vec_in, 16)
            act.wait_ge(zeroed, 1)
            nc.scalar.activation(cond[:, :, 0:ROWS], vec[:, V_COND:V_ALL].rearrange("p (k r) -> p k r", r=ROWS),
                                 ACT.Silu).then_inc(cond_ready, 1)
            for c in range(KD):
                square(0, c)
            root(0)
            def first_copy(c):
                act.wait_ge(ada_used, c + 1)
                if c:
                    act.wait_ge(ada_turned, c)
                nc.scalar.activation(ada_rows[:], ada_ps[:, c % 2, 0:2 * P], ACT.Copy).then_inc(ada_copied, 1)

            split_hi(0, 0, first=True)
            for c in range(KD):
                first_copy(c)
                if c:
                    round_hm(0, c - 1)
            split_hi(1, 1, first=True)
            round_hm(0, KD - 1)
            ada_load_first(2)

            def ada_next(s):
                ada_copy(s)
                ada_load_first(s + 1)

            ffn(0, 1, ({1: lambda: ada_last_quarter(2), 2: lambda: ada_next(2)},
                       {1: lambda: ada_last_quarter(3), 2: lambda: ada_next(3)},
                       {1: lambda: ada_last_quarter(4), 2: lambda: ada_next(4)}))
            ada_last_quarter(5)
            norm(1, MIX + 1)
            ada_copy(5)
            ada_load_first(6)
            act.wait_ge(wp_in, 16)
            act.wait_ge(tile_done[1], MIX)
            nc.scalar.activation(wp_hi[:], wp_raw[:], ACT.Copy).then_inc(wp_hi_ready, 1)
            def glu_gate(c):
                u = GLU[c]
                act.wait_ge(tile_done[0], u + 1)
                if c:
                    act.wait_ge(tile_read[1], GLU[c - 1] + 1)
                nc.scalar.activation(by_half(sil[:]), halves(tile_a), ACT.Sigmoid).then_inc(tile_read[0], 1)

            def pool_input(g):
                u, t = POOL_IN[g // 2], g % 2
                act.wait_ge(pads_ready, 1)
                act.wait_ge(state_in, 32)
                act.wait_ge(tile_done[t], u + 1)
                nc.scalar.activation(split2(pool_p[:, g, POOL_PAD:]), prompt(tiles[t]), ACT.Copy)
                nc.scalar.activation(split2(pool_s[:, g, POOL_PAD * DEC_BATCH:]), sample(tiles[t]),
                                     ACT.Copy).then_inc(tile_read[t], 1)

            def states_out():
                act.wait_ge(tile_read[0], OUT)
                act.wait_ge(tile_read[1], OUT)
                act.dma_start(conv_p_out, conv_p[:, :, SEQ:]).then_inc(state_out, 16)
                act.dma_start(conv_s_out, conv_s[:, :, DEC_SEQ * DEC_BATCH:]).then_inc(state_out, 16)
                act.dma_start(pool_p_out, pool_p[:, :, SEQ:]).then_inc(state_out, 16)
                act.dma_start(pool_s_out, pool_s[:, :, DEC_SEQ * DEC_BATCH:]).then_inc(state_out, 16)

            def pool_scale(g):
                w = WINDOWS[g]
                act.wait_ge(window_ready, g + 1)
                if g >= 2:
                    act.wait_ge(pooled_lo_ready, g - 1)
                s = sums[:, g % 2, :]
                m = by_half(mean_in[g % 2][:])
                nc.scalar.activation(prompt(m), split2(s[:, POOL_PAD:POOL_P]), ACT.Copy, scale=1.0 / w)
                nc.scalar.activation(sample(m), split2(s[:, POOL_P + POOL_PAD * DEC_BATCH:]), ACT.Copy,
                                     scale=1.0 / w).then_inc(scaled_ready, 1)

            def pool_round(g):
                act.wait_ge(pooled_ready, g + 1)
                if g >= 2:
                    act.wait_ge(pmix_done, g - 1)
                nc.scalar.activation(pooled_hi[:, g % 2, :], mean_in[g % 2][:], ACT.Copy).then_inc(pooled_hi_ready, 1)

            def pmix_read(g):
                act.wait_ge(pmix_done, g + 1)
                if g >= 2:
                    act.wait_ge(pmix_lo_ready, g - 1)
                nc.scalar.activation(by_half(full[:, g % 2, :]), halves(stat_ps), ACT.Copy,
                                     scale=col(V_PSC + g)).then_inc(pmix_full, 1)

            def pmix_round(g):
                act.wait_ge(pmix_full, g + 1)
                if g == 0:
                    act.wait_ge(tile_done[1], OUT)
                nc.scalar.activation(hm_hi[:, g, :], full[:, g % 2, :], ACT.Copy).then_inc(pmix_hi_ready, 1)

            def diagonals(b):
                if b == 0:
                    act.wait_ge(ident_ready, 1)
                for kk in range(TAPS_PER_LOOP):
                    if b:
                        act.wait_ge(diag_used, (b - 1) * TAPS_PER_LOOP + kk + 1)
                    w = V_WDW + (CONV_CHUNKS - 1) * WIDTH + PE_TAP0 + b * TAPS_PER_LOOP + kk
                    nc.scalar.activation(diag[:, kk, :], ident[:], ACT.Copy, scale=col(w)).then_inc(diag_ready, 1)

            glu_gate(0)
            split_hi(MIX + 2, 0)
            pool_input(0)
            pool_input(1)
            split_hi(MIX + 3, 1)
            glu_gate(1)
            diagonals(0)
            pool_scale(0)
            pool_round(0)
            split_hi(MIX + 4, 0)
            pool_scale(1)
            pool_input(2)
            pool_round(1)
            pool_input(3)
            split_hi(MIX + 5, 1)
            glu_gate(2)
            pool_scale(2)
            pmix_read(0)
            split_hi(OUT, 0)
            glu_gate(3)
            load_table(ACT.Sqrt)
            pool_round(2)
            split_hi(OUT + 1, 1)
            pmix_round(0)
            pmix_read(1)
            pmix_round(1)
            states_out()
            for a in range(ADA_QUARTERS * 7 - 1, ADA_QUARTERS * 7 + 1):
                ada_load(a)
            diagonals(1)
            pool_scale(3)
            ada_load(ADA_QUARTERS * 7 + 1)
            diagonals(2)
            pool_round(3)
            ada_copy(6)
            ada_load(ADA_QUARTERS * 7 + 2)
            diagonals(3)
            pmix_read(2)
            diagonals(4)
            pmix_round(2)
            pmix_read(3)
            pmix_round(3)
            for a in range(ADA_QUARTERS * 8 - 1, ADA_QUARTERS * 8 + 1):
                ada_load(a)
            act.wait_ge(pmix_lo_ready, GROUPS)
            for c in range(CONV_CHUNKS):
                act.wait_ge(ln_centred, c + 1)
                nc.scalar.activation(four[c], v[:, c, :], ACT.Square).then_inc(ln_sq_ready, 1)
            ada_load(ADA_QUARTERS * 8 + 1)
            act.wait_ge(ln_var_mm, 1)
            nc.scalar.activation(rms[:, 0, :], ln_sums_ps, ACT.Sqrt, scale=1.0 / D_CONV, bias=eps).then_inc(ln_std_ready, 1)
            load_table(ACT.Silu)
            ada_copy(7)
            ada_load(ADA_QUARTERS * 8 + 2)
            def vmix_round(c):
                act.wait_ge(vmix_full, c + 1)
                nc.scalar.activation(hm_hi[:, GROUPS + c, :], four[c], ACT.Copy).then_inc(vmix_hi_ready, 1)

            for c in range(CONV_CHUNKS):
                act.wait_ge(ln_scaled, c + 1)
                nc.scalar.activation(four[c], v[:, c, :], ACT.Silu, scale=col(V_LNG + c),
                                     bias=col(V_LNB + c)).then_inc(vmix_full, 1)
                if c:
                    vmix_round(c - 1)
            vmix_round(CONV_CHUNKS - 1)
            squares(2, OUT)
            ada_last_quarter(8)
            norm(2, FFN2 + 1)
            ada_copy(8)
            act.wait_ge(state_out, 16 * 4)
            ffn(1, 3, ({}, {}, {}))
            for c in Y_POOL:
                nc.scalar.activation(full[:, c % 2, :], x[:, c, :], ACT.Copy, scale=col(V_GF + c)).then_inc(y_scaled, 1)
                if c == Y_POOL[0]:
                    root(3)
            act.wait_ge(r_copy_ready, 1)
            nc.scalar.activation(mean_b[:], tile_a.rearrange("p h n -> p (h n)")[:, 0:TOKENS], ACT.Copy).then_inc(y_scaled, 1)

        @block.vector
        def _(dve):
            mod_steps = [0]

            def mod_evacuate(s):
                dve.wait_ge(ada_turned, copies(s))
                for j in range(2):
                    rows = ada_ps[:, s % 2, ADA_N + P * j:ADA_N + P * (j + 1)].rearrange("p (g r) -> p g r", g=4)[:, :, 0:ROWS]
                    bias = col(V_ADA + KD * s, KD).rearrange("p (g j) -> p g j", j=2)[:, :, j:j + 1]
                    ins = nc.vector.tensor_tensor(
                        mod[:, s].rearrange("p (g j) r -> p g j r", j=2)[:, :, j, :], rows,
                        bias.broadcast_to([P, 4, ROWS]), ALU.add)
                if s not in SCALE and s not in (GATE[0], GATE[2]):
                    ins.then_inc(mod_ready, 1)
                    dve.wait_ge(mod_ready, s - 1)
                    return
                ins.then_inc(mod_step, 1)
                mod_steps[0] += 1
                dve.wait_ge(mod_step, mod_steps[0])
                if s in SCALE:
                    n = SCALE.index(s)
                    g = col(V_G + KD * n, KD).unsqueeze(2).broadcast_to([P, KD, ROWS])
                    nc.vector.scalar_tensor_tensor(gain[:, n], mod[:, s], 1.0, g, ALU.add, ALU.mult).then_inc(mod_ready, 1)
                else:
                    nc.vector.tensor_scalar(mod[:, s], mod[:, s], 0.5, None, ALU.mult).then_inc(mod_ready, 1)
                dve.wait_ge(mod_ready, s - 1)

            def add_square(n, c):
                if 0 < c < KD - 1:
                    dve.wait_ge(sq_ready, KD * n + c + 1)
                if c == 1:
                    nc.vector.tensor_tensor(acc[:], sq[:, 0, :], sq[:, 1, :], ALU.add).then_inc(sq_used, 2)
                elif 1 < c < KD - 1:
                    dve.wait_ge(sq_used, (KD - 1) * n + c)
                    nc.vector.tensor_tensor(acc[:], acc[:], sq[:, c % 2, :], ALU.add).then_inc(sq_used, 1)

            def inverse(n):
                dve.wait_ge(std_ready, n + 1)
                nc.vector.reciprocal(rms[:, 1, :], rms[:, 0, :]).then_inc(rstd_ready, 1)

            def first_modulation(c):
                dve.wait_ge(ada_turned, c + 1)
                dve.wait_ge(vec_in, 16)
                for j in range(2):
                    nc.vector.tensor_scalar(mod[:, j, c, :], first_ps(c, j), col(V_ADA + KD * j + c), None,
                                            ALU.add).then_inc(first_added, 1)
                dve.wait_ge(first_added, 2 * (c + 1))
                ins = nc.vector.tensor_scalar(gain[:, 0, c, :], mod[:, 1, c, :], 1.0, col(V_G + c), ALU.add, ALU.mult)
                ins.then_inc(first_ready, 1)
                dve.wait_ge(first_ready, c + 1)

            def apply_norm(n):
                dve.wait_ge(r_ready, n + 1)
                r = by_half(r_ps)

                def scale_samples(c):
                    if c >= 2:
                        dve.wait_ge(norm_fs, KD * n + c - 1)
                    nc.vector.tensor_tensor(sample(by_half(sq[:, c % 2, :])), sample(by_half(x[:, c, :])), sample(r),
                                            ALU.mult).then_inc(norm_s1, 1)

                def low(c):
                    dve.wait_ge(hm_hi_ready, KD * n + c + 1)
                    nc.vector.tensor_tensor(hm_lo[:, c, :], full[:, c % 2, :], hm_hi[:, c, :].bitcast(F32),
                                            ALU.subtract).then_inc(hm_lo_ready[c % 2], 1)

                scale_samples(0)
                for c in range(KD):
                    if n == 0 and c % 2:
                        low(c - 1)
                    if n == 0:
                        first_modulation(c)
                    q = KD * n + c
                    t, f = by_half(sq[:, c % 2, :]), by_half(full[:, c % 2, :])
                    if c >= 2:
                        dve.wait_ge(norm_f, q - 1)
                    nc.vector.scalar_tensor_tensor(prompt(t), prompt(by_half(x[:, c, :])), gain[:, n, c, 0:1],
                                                   prompt(r), ALU.mult, ALU.mult).then_inc(norm_t, 1)
                    dve.wait_ge(norm_s1, q + 1)
                    nc.vector.tensor_tensor(steps(sample(t)), steps(sample(t)), over_steps(gain[:, n, c, 1:ROWS]),
                                            ALU.mult).then_inc(norm_s2, 1)
                    if c + 1 < KD:
                        scale_samples(c + 1)
                    if c >= 2:
                        dve.wait_ge(*lo_at(n, c - 2))
                    dve.wait_ge(norm_s2, q + 1)
                    nc.vector.tensor_tensor(steps(sample(f)), steps(sample(t)),
                                            over_steps(mod[:, SHIFT[n], c, 1:ROWS]), ALU.add).then_inc(norm_fs, 1)
                    if n and c % 2:
                        low(c - 1)
                if n == 0:
                    low(KD - 1)

            def up_unit(u, side, local, before):
                dve.wait_ge(tile_done[1], u + 1)
                dve.wait_ge(tile_read[0], u + 1)
                nc.vector.tensor_tensor(by_half(full[:, side, :]), by_half(sil[:]), halves(tile_b),
                                        ALU.mult).then_inc(tile_read[1], 1)
                dve.wait_ge(h_hi_ready, before + local + 1)
                nc.vector.tensor_tensor(h_lo[:, local, :], full[:, side, :], h_hi[:, local, :].bitcast(F32),
                                        ALU.subtract).then_inc(h_lo_ready, 1)

            def residual(u, m, t, e, s):
                ps = tiles[t]
                xm = by_half(x[:, m, :]) if isinstance(m, int) else by_half(x[:, bass.ds(m, 1), :].rearrange("p o n -> p (o n)"))
                dve.wait_ge(tile_done[t], u + 1)
                g = steps(gated[:, t, :].rearrange("p (h n) -> p h n", h=2))
                nc.vector.tensor_tensor(g, steps(sample(ps)), over_steps(gate_rows(s, m)), ALU.mult).then_inc(gate_tmp, 1)
                nc.vector.scalar_tensor_tensor(prompt(xm), prompt(ps), gate_prompt(s, m), prompt(xm), ALU.mult,
                                               ALU.add).then_inc(tile_read[t], 1)
                dve.wait_ge(gate_tmp, e + 1)
                nc.vector.tensor_tensor(steps(sample(xm)), steps(sample(xm)), g, ALU.add).then_inc(x_ready, 1)

            def gate_rows(s, m):
                return mod[:, s, m, 1:ROWS] if isinstance(m, int) else mod[:, s, bass.ds(m, 1), 1:ROWS].rearrange("p o r -> p (o r)")

            def gate_prompt(s, m):
                return mod[:, s, m, 0:1] if isinstance(m, int) else mod[:, s, bass.ds(m, 1), 0:1].rearrange("p o r -> p (o r)")

            def down_unit(u, i, e0, s):
                for t in range(2):
                    residual(u, i * 2 + t, t, e0 + i * 2 + t, s)

            def down_and_squares(first_unit, e0, s, n):
                for i in range(KD // 2):
                    u = first_unit + i
                    residual(u, 2 * i, 0, e0 + 2 * i, s)
                    add_square(n, 2 * i)
                    residual(u, 2 * i + 1, 1, e0 + 2 * i + 1, s)
                    add_square(n, 2 * i + 1)

            def ffn(f, gate, norm_after, between):
                for part, n, up, down, before, e0 in FFNS[f]:
                    pairs_and(dve, n, lambda i, side: up_unit(up + i, side, i, before), between[part])
                    if part < len(FF_PARTS) - 1:
                        pairs(dve, KD // 2, lambda i, side: down_unit(down + i, i, e0, gate))
                    else:
                        down_and_squares(down, e0, gate, norm_after)
                inverse(norm_after)

            for c in range(KD):
                add_square(0, c)
            inverse(0)
            apply_norm(0)
            dve.wait_ge(w_hi_ready, 2)
            nc.vector.tensor_tensor(w_lo[:, 1, UNIT // 2:], w_raw[:, 1, UNIT // 2:],
                                    w_hi[:, 1, UNIT // 2:].bitcast(F32), ALU.subtract).then_inc(w1_half_ready, 1)
            ffn(0, GATE[0], 1, ({4: lambda: mod_evacuate(2)}, {4: lambda: mod_evacuate(3)}, {3: lambda: mod_evacuate(4)}))
            apply_norm(1)

            def glu(c):
                u = GLU[c]
                if c == 0:
                    dve.wait_ge(pads_ready, 1)
                    dve.wait_ge(state_in, 32)
                dve.wait_ge(tile_read[0], u + 1)
                dve.wait_ge(tile_done[1], u + 1)
                s = by_half(sil[:])
                nc.vector.tensor_tensor(split2(conv_p[:, c, CONV_PAD:]), prompt(s), prompt(tile_b),
                                        ALU.mult)
                nc.vector.tensor_tensor(split2(conv_s[:, c, CONV_PAD * DEC_BATCH:]), sample(s), sample(tile_b),
                                        ALU.mult).then_inc(tile_read[1], 1)

            def window(c, k):
                if isinstance(k, int):
                    return (split2(conv_p[:, c, k:k + SEQ]),
                            split2(conv_s[:, c, DEC_BATCH * k:DEC_BATCH * (k + DEC_SEQ)]), col(V_WDW + c * WIDTH + k))
                return (split2(conv_p[:, c, bass.ds(k, SEQ)]),
                        split2(conv_s[:, c, bass.ds(k * DEC_BATCH, DEC_BATCH * DEC_SEQ)]),
                        vec[:, bass.ds(k + (V_WDW + c * WIDTH), 1)])

            def conv_start(c):
                vc = by_half(v[:, c, :])
                win_p, win_s, w = window(c, 0)
                dve.wait_ge(tile_read[1], GLU[c] + 1)
                nc.vector.tensor_scalar(prompt(vc), win_p, w, col(V_BDW + c), ALU.mult, ALU.add).then_inc(conv_tap, 1)
                nc.vector.tensor_scalar(sample(vc), win_s, w, col(V_BDW + c), ALU.mult, ALU.add).then_inc(conv_tap, 1)

            def conv_taps(c, g0, g1):
                vc = by_half(v[:, c, :])
                with dve.Fori(g0, g1) as g:
                    for kk in range(TAPS_PER_LOOP):
                        k = g * TAPS_PER_LOOP + (kk + 1)
                        done = g * (2 * TAPS_PER_LOOP) + 2 * (kk + 1 + c * WIDTH)
                        win_p, win_s, w = window(c, k)
                        dve.wait_ge(conv_tap, done - 1)
                        nc.vector.scalar_tensor_tensor(prompt(vc), win_p, w, prompt(vc), ALU.mult,
                                                       ALU.add).then_inc(conv_tap, 1)
                        dve.wait_ge(conv_tap, done)
                        nc.vector.scalar_tensor_tensor(sample(vc), win_s, w, sample(vc), ALU.mult,
                                                       ALU.add).then_inc(conv_tap, 1)

            glu(0)
            mod_evacuate(5)
            conv_start(0)
            conv_taps(0, 0, TAP_GROUPS - 1)
            glu(1)
            conv_taps(0, TAP_GROUPS - 1, TAP_GROUPS)
            conv_start(1)
            conv_taps(1, 0, TAP_GROUPS - 2)
            glu(2)
            conv_taps(1, TAP_GROUPS - 2, TAP_GROUPS)
            glu(3)
            conv_start(2)
            conv_taps(2, 0, TAP_GROUPS)
            mod_evacuate(6)
            conv_start(3)
            conv_taps(3, 0, TAP_GROUPS - PE_BATCHES)
            dve.wait_ge(diag_used, WIDTH - PE_TAP0)
            dve.wait_ge(conv_tap, 2 * DVE_TAPS)
            vc = by_half(v[:, CONV_CHUNKS - 1, :])
            nc.vector.tensor_tensor(prompt(vc), prompt(vc), split2(tile_a[:, 0, 0:SEQ]), ALU.add).then_inc(pe_taps_added, 1)
            nc.vector.tensor_tensor(sample(vc), sample(vc), split2(tile_a[:, 1, 0:DEC_BATCH * DEC_SEQ]),
                                    ALU.add).then_inc(pe_taps_added, 1)
            dve.wait_ge(ln_sum_done, 1)
            for c in range(CONV_CHUNKS):
                vc = by_half(v[:, c, :])
                nc.vector.scalar_tensor_tensor(vc, halves(stat_ps), -1.0 / D_CONV, vc, ALU.mult,
                                               ALU.add).then_inc(ln_centred, 1)
            for c in range(1, CONV_CHUNKS - 1):
                dve.wait_ge(ln_sq_ready, c + 1)
                if c == 1:
                    dve.wait_ge(pooled_lo_ready, GROUPS)
                else:
                    dve.wait_ge(ln_sq_added, c - 1)
                nc.vector.tensor_tensor(acc[:], acc[:] if c > 1 else four[0], four[c], ALU.add).then_inc(ln_sq_added, 1)
            dve.wait_ge(ln_std_ready, 1)
            nc.vector.reciprocal(rms[:, 1, :], rms[:, 0, :]).then_inc(ln_rstd_ready, 1)
            dve.wait_ge(ln_r_ready, 1)
            for c in range(CONV_CHUNKS):
                nc.vector.tensor_tensor(v[:, c, :], v[:, c, :], r_ps, ALU.mult).then_inc(ln_scaled, 1)
            for c in range(CONV_CHUNKS):
                dve.wait_ge(vmix_hi_ready, c + 1)
                nc.vector.tensor_tensor(hm_lo[:, GROUPS + c, :], four[c],
                                        hm_hi[:, GROUPS + c, :].bitcast(F32), ALU.subtract).then_inc(vmix_lo_ready, 1)
            mod_evacuate(7)
            down_and_squares(OUT, OUT_TILES, GATE[1], 2)
            inverse(2)
            apply_norm(2)
            ffn(1, GATE[2], 3, ({1: lambda: mod_evacuate(8)}, {}, {}))
            dve.wait_ge(r_ready, 4)
            for c in range(Y_POOL[0]):
                nc.vector.scalar_tensor_tensor(x[:, c, :], x[:, c, :], col(V_GF + c), r_ps, ALU.mult,
                                               ALU.mult).then_inc(y_ready, 1)

        @block.gpsimd
        def _(pool):
            def split_lo(u, side):
                pool.wait_ge(w_hi_ready, u + 1)
                nc.gpsimd.tensor_tensor(w_lo[:, side, :], w_raw[:, side, :], w_hi[:, side, :].bitcast(F32),
                                        ALU.subtract).then_inc(w_lo_ready, 1)

            def hm_lows(n, next_unit):
                side = next_unit % 2

                def part(first, last):
                    cols = slice(first, last)
                    return nc.gpsimd.tensor_tensor(w_lo[:, side, cols], w_raw[:, side, cols],
                                                   w_hi[:, side, cols].bitcast(F32), ALU.subtract)

                if n:
                    pool.wait_ge(w_hi_ready, next_unit + 1)
                    part(0, UNIT // 2)
                for c in range(1, KD if n else KD - 2, 2):
                    pool.wait_ge(hm_hi_ready, KD * n + c + 1)
                    nc.gpsimd.tensor_tensor(hm_lo[:, c, :], full[:, c % 2, :], hm_hi[:, c, :].bitcast(F32),
                                            ALU.subtract).then_inc(hm_lo_ready[1], 1)
                if n:
                    part(UNIT // 2, UNIT).then_inc(w_lo_ready, 1)
                else:
                    pool.wait_ge(w_hi_ready, 2)
                    part(0, 3 * UNIT // 8)
                    pool.wait_ge(w1_half_ready, 1)
                    part(3 * UNIT // 8, UNIT // 2).then_inc(w_lo_ready, 1)

            def split_pairs(first, last):
                with pool.Fori(first // 2, last // 2) as i:
                    for side in range(2):
                        split_lo(i * 2 + side, side)

            nc.gpsimd.memset(cond[:], 0.0).then_inc(zeroed, 1)
            nc.gpsimd.memset(ident[:], 0.0).then_inc(ident_zero, 1)
            nc.gpsimd.memset(ones[:], 1.0)
            for t in range(POOL_PAD):
                nc.gpsimd.memset(small[:, t:t + 1], 1.0 / (t + 1))
            nc.gpsimd.memset(scrap, 0.0)
            nc.gpsimd.memset(eps, EPS).then_inc(consts_ready, 1)
            pool.wait_ge(ident_zero, 1)
            nc.gpsimd.affine_select(out=ident[:], in_=ident[:], compare_op=ALU.not_equal, fill=1.0, base=0,
                                    pattern=[[-1, P]], channel_multiplier=1).then_inc(ident_ready, 1)
            pool.wait_ge(ident_ready, 1)
            nc.gpsimd.tensor_tensor(sel[:, 1:3, :], split2(ident[:, 0:P // 2]), split2(ident[:, P // 2:]),
                                    ALU.add).then_inc(sel_step, 1)
            pool.wait_ge(sel_step, 1)
            nc.gpsimd.tensor_tensor(sel[:, 0, :], sel[:, 1, :], sel[:, 2, :], ALU.add).then_inc(sel_ready, 1)
            split_lo(0, 0)
            hm_lows(0, 1)
            split_pairs(2, MIX)
            split_lo(MIX, 0)
            hm_lows(1, MIX + 1)
            pool.wait_ge(tile_done[1], MIX)
            nc.gpsimd.memset(conv_p[:, :, 0:CONV_PAD], 0.0)
            nc.gpsimd.memset(pool_p[:, :, 0:POOL_PAD], 0.0).then_inc(pads_ready, 1)
            split_lo(MIX + 2, 0)
            pool.wait_ge(wp_hi_ready, 1)
            nc.gpsimd.tensor_tensor(wp_lo[:], wp_raw[:], wp_hi[:].bitcast(F32), ALU.subtract).then_inc(wp_lo_ready, 1)

            def window_sums(g):
                pool.wait_ge(tile_read[g % 2], POOL_IN[g // 2] + 1)
                src_p, src_s = pool_p[:, g, :], pool_s[:, g, :]
                for level in range(g + 1):
                    d = 1 << level
                    first = 2 * d - 1
                    dst = sums[:, level % 2, :]
                    dst_p, dst_s = dst[:, 0:POOL_P], dst[:, POOL_P:]
                    if level:
                        pool.wait_ge(pool_step, steps_done[0])
                    nc.gpsimd.tensor_tensor(dst_p[:, first:POOL_P], src_p[:, first:POOL_P],
                                            src_p[:, first - d:POOL_P - d], ALU.add)
                    a, b, n = first * DEC_BATCH, (first - d) * DEC_BATCH, POOL_S - first * DEC_BATCH
                    ins = nc.gpsimd.tensor_tensor(dst_s[:, a:a + n], src_s[:, a:a + n], src_s[:, b:b + n], ALU.add)
                    if level < g:
                        ins.then_inc(pool_step, 1)
                        steps_done[0] += 1
                    else:
                        ins.then_inc(window_ready, 1)
                    src_p, src_s = dst_p, dst_s

            def window_means(g):
                pool.wait_ge(window_ready, g + 1)
                pool.wait_ge(scaled_ready, g + 1)
                m = mean_in[g % 2]
                n = WINDOWS[g] - 1
                nc.gpsimd.tensor_tensor(m[:, 0:n], sums[:, g % 2, POOL_PAD:POOL_PAD + n], small[:, 0:n],
                                        ALU.mult).then_inc(pool_step, 1)
                steps_done[0] += 1
                pool.wait_ge(pool_step, steps_done[0])
                mh = by_half(m[:])
                nc.gpsimd.tensor_tensor(prompt(mh), prompt(mh), split2(pool_p[:, g, POOL_PAD:]), ALU.subtract)
                nc.gpsimd.tensor_tensor(sample(mh), sample(mh), split2(pool_s[:, g, POOL_PAD * DEC_BATCH:]),
                                        ALU.subtract).then_inc(pooled_ready, 1)
                pool.wait_ge(pooled_hi_ready, g + 1)
                nc.gpsimd.tensor_tensor(pooled_lo[:, g % 2, :], m[:], pooled_hi[:, g % 2, :].bitcast(F32),
                                        ALU.subtract).then_inc(pooled_lo_ready, 1)

            steps_done = [0]
            split_lo(MIX + 3, 1)
            for g in range(GROUPS):
                window_sums(g)
                if g:
                    split_lo((MIX + 4, OUT, OUT + 1)[g - 1], (0, 0, 1)[g - 1])
                window_means(g)
                if g == 1:
                    split_lo(MIX + 5, 1)
            for g in range(GROUPS):
                pool.wait_ge(pmix_hi_ready, g + 1)
                nc.gpsimd.tensor_tensor(hm_lo[:, g, :], full[:, g % 2, :], hm_hi[:, g, :].bitcast(F32),
                                        ALU.subtract).then_inc(pmix_lo_ready, 1)
            for u in range(OUT + 2, FFN2 + 1):
                split_lo(u, u % 2)
            hm_lows(2, FFN2 + 1)
            split_pairs(FFN2 + 2, UNITS)
            pool.wait_ge(y_scaled, len(Y_POOL) + 1)
            for c in Y_POOL:
                nc.gpsimd.tensor_tensor(x[:, c, :], full[:, c % 2, :], mean_b[:], ALU.mult).then_inc(y_pool_ready, 1)


def column_units(w, tiles):
    import numpy as np

    k = w.shape[0] // P
    blocks = w.reshape(k, P, w.shape[1] // P, P)
    out = np.zeros((len(tiles), P, UNIT), w.dtype)
    for n, (a, b) in enumerate(tiles):
        both = np.stack([blocks[:, :, a], blocks[:, :, b]], axis=1)
        out[n, :, :2 * k * P] = both.transpose(2, 0, 1, 3).reshape(P, 2 * k * P)
    return out


def ffn_units(up, down):
    import numpy as np

    n_hidden, first, units = D_FF // P, 0, []
    pairs_out = [(m, m + 1) for m in range(0, KD, 2)]
    for n in FF_PARTS:
        units.append(column_units(up, [(f, n_hidden + f) for f in range(first, first + n)]))
        units.append(column_units(down[first * P:(first + n) * P], pairs_out))
        first += n
    return np.concatenate(units)


def to_halves(xp, xs):
    import numpy as np

    steps = xs.transpose(1, 0, 2).reshape(2, HALF_STEPS * DEC_BATCH, -1)
    both = np.concatenate([xp.reshape(2, HALF_PROMPT, -1), steps], axis=1)
    return both.reshape(TOKENS, -1).T


def chunks(a):
    return a.reshape(a.shape[0] // P, P, *a.shape[1:]).swapaxes(0, 1)


def kernel(**inputs):
    import numpy as np
    import concourse.bacc as bacc
    from concourse.bass_utils import run_bass_kernel_spmd

    a = {k: np.asarray(t) for k, t in inputs.items()}
    pairs_out = [(m, m + 1) for m in range(0, KD, 2)]
    w_in = a["w_in"][0]
    mixed_rows = np.concatenate([a["w_out"][0][D_CONV:], a["w_out"][0][:D_CONV]])
    mixer_tiles = [None] * (OUT - MIX)
    for c, u in enumerate(GLU):
        mixer_tiles[u - MIX] = (CONV_CHUNKS + c, c)
    for n, u in enumerate(POOL_IN):
        mixer_tiles[u - MIX] = (2 * (CONV_CHUNKS + n), 2 * (CONV_CHUNKS + n) + 1)
    units = np.concatenate([
        ffn_units(a["w_ffn1_up"][0], a["w_ffn1_down"][0]),
        column_units(w_in, mixer_tiles),
        column_units(mixed_rows, pairs_out),
        ffn_units(a["w_ffn2_up"][0], a["w_ffn2_down"][0])])
    w_ada = a["w_ada"][0].reshape(ADA_QUARTERS, 2, P, N_MOD, D_MODEL).transpose(3, 0, 2, 1, 4)
    w_ada = w_ada.reshape(N_MOD * ADA_QUARTERS, P, 2, D_MODEL).copy()
    first = a["w_ada"][0].reshape(KD, P, N_MOD, KD, P)[:, :, :2].transpose(3, 1, 0, 2, 4)
    w_ada[:KD] = first.reshape(KD, P, 2, D_MODEL)
    cond = np.concatenate([a["c_prompt"], a["c_sample"]])
    vectors = np.concatenate(
        [chunks(a["b_ada"][0])] + [chunks(a[n][0]) for n in ("g_ffn1", "g_mix", "g_ffn2")] + [chunks(a["g_final"])]
        + [chunks(a[n][0]) for n in ("ln_g", "ln_b", "b_dw", "pool_scale")]
        + [chunks(a["w_dw"][0].T).reshape(P, -1), chunks(cond.T).reshape(P, -1)], axis=1)
    arrays = {
        "x_in": chunks(to_halves(a["x_prompt"][0], a["x_sample"])),
        "w_units": units,
        "w_ada": w_ada,
        "w_pool": a["w_pool"][0].transpose(1, 0, 2).reshape(P, GROUPS * P),
        "vectors": vectors,
        "conv_state": chunks(a["state_conv"][0].transpose(2, 1, 0).reshape(D_CONV, -1)),
        "pool_state": chunks(a["state_pool"][0].transpose(2, 1, 0).reshape(D_POOL, -1)),
    }
    arrays = {k: np.ascontiguousarray(t) for k, t in arrays.items()}
    outs = {"y_out": (P, KD, TOKENS), "conv_p_out": (P, CONV_CHUNKS, CONV_PAD), "pool_p_out": (P, GROUPS, POOL_PAD),
            "conv_s_out": (P, CONV_CHUNKS, CONV_PAD * DEC_BATCH), "pool_s_out": (P, GROUPS, POOL_PAD * DEC_BATCH)}
    nc = bacc.Bacc("TRN2", target_bir_lowering=False, num_devices=1)
    args = [nc.dram_tensor(k, t.shape, mybir.dt.from_np(t.dtype), kind="ExternalInput").ap() for k, t in arrays.items()]
    args += [nc.dram_tensor(k, s, F32, kind="ExternalOutput").ap() for k, s in outs.items()]
    trunk(nc, *args)
    got = run_bass_kernel_spmd(nc, [arrays], core_ids=[0]).results[0]

    def rows(name):
        t = np.asarray(got[name])
        return t.transpose(2, 1, 0).reshape(t.shape[2], -1)

    y = rows("y_out").reshape(2, HALF, D_MODEL)
    y_sample = y[:, HALF_PROMPT:].reshape(DEC_SEQ, DEC_BATCH, D_MODEL).swapaxes(0, 1)
    return (np.ascontiguousarray(y[:, :HALF_PROMPT].reshape(1, SEQ, D_MODEL)),
            np.ascontiguousarray(y_sample),
            np.ascontiguousarray(rows("conv_p_out")[None, None]),
            np.ascontiguousarray(rows("pool_p_out")[None, None]),
            np.ascontiguousarray(rows("conv_s_out").reshape(CONV_PAD, DEC_BATCH, D_CONV).swapaxes(0, 1)[None]),
            np.ascontiguousarray(rows("pool_s_out").reshape(POOL_PAD, DEC_BATCH, D_POOL).swapaxes(0, 1)[None]))
```
